# Optimizing a Trainium2 kernel written in Bass

```python
import math
import jax, jax.numpy as jnp
from jax import lax
import numpy as np

D_MODEL = 1024
BATCH = 1
SEQ = 128
DEPTH = 1
DEC_BATCH = 1
DEC_SEQ = 256
PAST_LEN = 128

GRID_W = 64
N_HEADS = 16
QK_NOPE_DIM = 64
QK_ROPE_DIM = 32
V_DIM = 64
Q_LORA = 384
KV_LORA = 256
ROPE_BASE = 10000.0
Q_BLOCK = 128
ATTN_SCALE = 1.0 / math.sqrt(QK_NOPE_DIM + QK_ROPE_DIM)
CONV_C = D_MODEL
CONV_K = 31
CONV_PAD = CONV_K // 2
N_EXPERTS = 64
TOP_K = 8
N_GROUPS = 8
TOPK_GROUPS = 4
EXPERT_FF = 256
ROUTED_SCALE = 2.5
EPS = 1e-6
N_MOD = 6
IN_COLS = Q_LORA + KV_LORA + QK_ROPE_DIM + 2 * CONV_C + 2 * D_MODEL
SPLITS = [Q_LORA, Q_LORA + KV_LORA, Q_LORA + KV_LORA + QK_ROPE_DIM,
          Q_LORA + KV_LORA + QK_ROPE_DIM + 2 * CONV_C]

kernel_name = "hybrid_mla_conformer_moe_dit_step"

def rmsnorm(x, g):
    xf = x.astype(jnp.float32)
    y = xf * lax.rsqrt(jnp.mean(xf * xf, axis=-1, keepdims=True) + EPS)
    return (y * g.astype(jnp.float32)).astype(x.dtype)

def layernorm(x, g, b):
    xf = x.astype(jnp.float32)
    mu = jnp.mean(xf, axis=-1, keepdims=True)
    var = jnp.mean(jnp.square(xf - mu), axis=-1, keepdims=True)
    y = (xf - mu) * lax.rsqrt(var + EPS)
    return (y * g.astype(jnp.float32) + b.astype(jnp.float32)).astype(x.dtype)

def axial_rope(seq_len):
    pos = jnp.arange(seq_len, dtype=jnp.int32)
    row = (pos // GRID_W).astype(jnp.float32)
    col = (pos % GRID_W).astype(jnp.float32)
    n_freq = QK_ROPE_DIM // 4
    inv_freq = ROPE_BASE ** (-jnp.arange(n_freq, dtype=jnp.float32) / n_freq)
    ang = jnp.stack([row[:, None] * inv_freq, col[:, None] * inv_freq], axis=1)
    return jnp.cos(ang), jnp.sin(ang)

def apply_rope(x, cos, sin):
    shp = x.shape
    xr = x.reshape(*shp[:-1], 2, 2, shp[-1] // 4)
    x1, x2 = xr[..., 0, :], xr[..., 1, :]
    c = cos[:, None].astype(x.dtype)
    s = sin[:, None].astype(x.dtype)
    out = jnp.stack([x1 * c - x2 * s, x1 * s + x2 * c], axis=-2)
    return out.reshape(shp)

def adaln(cond, w, b):
    m = (jax.nn.silu(cond) @ w + b)[:, None, :]
    return jnp.split(m, N_MOD, axis=-1)

def decompress_kv(ckv, w_ukv):
    B, S, _ = ckv.shape
    kv = (ckv @ w_ukv).reshape(B, S, N_HEADS, QK_NOPE_DIM + V_DIM)
    return kv[..., :QK_NOPE_DIM], kv[..., QK_NOPE_DIM:]

def mla_attend(q_nope, q_rope, k_nope, k_rope, v):
    B, S, H, _ = q_nope.shape
    nb = S // Q_BLOCK

    def block(args):
        qn, qr = args
        s = (jnp.einsum('bqhd,bkhd->bhqk', qn, k_nope)
             + jnp.einsum('bqhr,bkr->bhqk', qr, k_rope)).astype(jnp.float32)
        p = jax.nn.softmax(s * ATTN_SCALE, axis=-1).astype(v.dtype)
        return jnp.einsum('bhqk,bkhd->bqhd', p, v)

    qn_b = q_nope.reshape(B, nb, Q_BLOCK, H, QK_NOPE_DIM).transpose(1, 0, 2, 3, 4)
    qr_b = q_rope.reshape(B, nb, Q_BLOCK, H, QK_ROPE_DIM).transpose(1, 0, 2, 3, 4)
    out = lax.map(block, (qn_b, qr_b))
    return out.transpose(1, 0, 2, 3, 4).reshape(B, S, H * V_DIM)

def conformer_conv(u, conv_w, conv_b, ln_g, ln_b, w_pw2):
    a, g = jnp.split(u, 2, axis=-1)
    z = a * jax.nn.sigmoid(g)
    z = lax.conv_general_dilated(z, conv_w[:, None, :].astype(z.dtype), window_strides=(1,),
                                 padding=[(CONV_PAD, CONV_PAD)],
                                 dimension_numbers=('NWC', 'WIO', 'NWC'),
                                 feature_group_count=CONV_C) + conv_b
    z = jax.nn.silu(layernorm(z, ln_g, ln_b))
    return z @ w_pw2

def moe(h, router_w, router_bias, exp_w_gate, exp_w_up, exp_w_down, sh_w_gate, sh_w_up, sh_w_down):
    B, S, D = h.shape
    t = h.reshape(B * S, D)
    T = t.shape[0]
    scores = jax.nn.sigmoid((t @ router_w).astype(jnp.float32))
    sel = scores + router_bias.astype(jnp.float32)
    grp = sel.reshape(T, N_GROUPS, N_EXPERTS // N_GROUPS)
    grp_score = jnp.sum(lax.top_k(grp, 2)[0], axis=-1)
    _, gidx = lax.top_k(grp_score, TOPK_GROUPS)
    gmask = jnp.sum(jax.nn.one_hot(gidx, N_GROUPS, dtype=jnp.float32), axis=1)
    emask = jnp.repeat(gmask, N_EXPERTS // N_GROUPS, axis=1)
    masked = jnp.where(emask > 0, sel, -jnp.inf)
    _, idx = lax.top_k(masked, TOP_K)
    w = jnp.take_along_axis(scores, idx, axis=-1)
    w = w / jnp.sum(w, axis=-1, keepdims=True) * ROUTED_SCALE
    gates = jnp.sum(jax.nn.one_hot(idx, N_EXPERTS, dtype=jnp.float32) * w[..., None], axis=1)
    hid = jax.nn.silu(jnp.einsum('td,edf->tef', t, exp_w_gate)) * jnp.einsum('td,edf->tef', t, exp_w_up)
    hid = hid * gates[:, :, None].astype(hid.dtype)
    routed = jnp.einsum('tef,efd->td', hid, exp_w_down)
    shared = (jax.nn.silu(t @ sh_w_gate) * (t @ sh_w_up)) @ sh_w_down
    return (routed + shared).reshape(B, S, D)

def trunk_layer(x, mods, lp, rope, ctx_kv):
    shift1, scale1, gate1, shift2, scale2, gate2 = mods
    B, S, _ = x.shape
    h = rmsnorm(x, lp['norm1_g']) * (1.0 + scale1) + shift1
    u = h @ lp['w_in']
    q_lat, ckv, k_rope, conv_in, gate_logits = jnp.split(u, SPLITS, axis=-1)
    q = (rmsnorm(q_lat, lp['q_norm_g']) @ lp['w_uq']).reshape(B, S, N_HEADS, QK_NOPE_DIM + QK_ROPE_DIM)
    q_nope, q_rope = q[..., :QK_NOPE_DIM], q[..., QK_NOPE_DIM:]
    ckv = rmsnorm(ckv, lp['kv_norm_g'])
    k_nope, v = decompress_kv(ckv, lp['w_ukv'])
    k_rope_used = k_rope
    if rope is not None:
        cos, sin = rope
        q_rope = apply_rope(q_rope, cos, sin)
        k_rope_used = apply_rope(k_rope[:, :, None, :], cos, sin)[:, :, 0, :]
    if ctx_kv is not None:
        ckv_ctx, krope_ctx = ctx_kv
        kn_ctx, v_ctx = decompress_kv(ckv_ctx, lp['w_ukv'])
        k_nope = jnp.concatenate([k_nope, kn_ctx], axis=1)
        v = jnp.concatenate([v, v_ctx], axis=1)
        k_rope_used = jnp.concatenate([k_rope_used, krope_ctx], axis=1)
    attn_out = mla_attend(q_nope, q_rope, k_nope, k_rope_used, v) @ lp['w_o_attn']
    conv_out = conformer_conv(conv_in, lp['conv_w'], lp['conv_b'], lp['conv_ln_g'], lp['conv_ln_b'], lp['w_pw2'])
    g_attn, g_conv = jnp.split(jax.nn.sigmoid(gate_logits), 2, axis=-1)
    mix = (g_attn * attn_out + g_conv * conv_out) @ lp['w_out']
    x = x + gate1 * mix
    h2 = rmsnorm(x, lp['norm2_g']) * (1.0 + scale2) + shift2
    ff = moe(h2, lp['router_w'], lp['router_bias'], lp['exp_w_gate'], lp['exp_w_up'], lp['exp_w_down'],
             lp['sh_w_gate'], lp['sh_w_up'], lp['sh_w_down'])
    x = x + gate2 * ff
    return x, ckv, k_rope

def setup_inputs(seed: int = 0) -> dict:
    key = jax.random.key(seed)
    ks = iter(jax.random.split(key, 40))

    def nrm(shape, scale=1.0):
        return jax.random.normal(next(ks), shape, jnp.float32) * scale

    def gain(shape):
        return 1.0 + 0.05 * jax.random.normal(next(ks), shape, jnp.float32)

    L, D = DEPTH, D_MODEL
    return {
        'x_prompt': nrm((BATCH, SEQ, D)),
        'x_sample': nrm((DEC_BATCH, DEC_SEQ, D)),
        'cache_ckv': nrm((DEC_BATCH, L, PAST_LEN, KV_LORA)),
        'cache_krope': nrm((DEC_BATCH, L, PAST_LEN, QK_ROPE_DIM)),
        'c': nrm((DEC_BATCH, D)),
        'c_ctx': nrm((D,)),
        'mod_w': nrm((L, D, N_MOD * D), 0.5 * D ** -0.5),
        'mod_b': nrm((L, N_MOD * D), 0.02),
        'norm1_g': gain((L, D)),
        'w_in': nrm((L, D, IN_COLS), D ** -0.5),
        'q_norm_g': gain((L, Q_LORA)),
        'w_uq': nrm((L, Q_LORA, N_HEADS * (QK_NOPE_DIM + QK_ROPE_DIM)), Q_LORA ** -0.5),
        'kv_norm_g': gain((L, KV_LORA)),
        'w_ukv': nrm((L, KV_LORA, N_HEADS * (QK_NOPE_DIM + V_DIM)), KV_LORA ** -0.5),
        'w_o_attn': nrm((L, N_HEADS * V_DIM, D), (N_HEADS * V_DIM) ** -0.5),
        'conv_w': nrm((L, CONV_K, CONV_C), CONV_K ** -0.5),
        'conv_b': nrm((L, CONV_C), 0.02),
        'conv_ln_g': gain((L, CONV_C)),
        'conv_ln_b': nrm((L, CONV_C), 0.02),
        'w_pw2': nrm((L, CONV_C, D), CONV_C ** -0.5),
        'w_out': nrm((L, D, D), D ** -0.5),
        'norm2_g': gain((L, D)),
        'router_w': nrm((L, D, N_EXPERTS), D ** -0.5),
        'router_bias': nrm((L, N_EXPERTS), 0.01),
        'exp_w_gate': nrm((L, N_EXPERTS, D, EXPERT_FF), D ** -0.5),
        'exp_w_up': nrm((L, N_EXPERTS, D, EXPERT_FF), D ** -0.5),
        'exp_w_down': nrm((L, N_EXPERTS, EXPERT_FF, D), EXPERT_FF ** -0.5),
        'sh_w_gate': nrm((L, D, EXPERT_FF), D ** -0.5),
        'sh_w_up': nrm((L, D, EXPERT_FF), D ** -0.5),
        'sh_w_down': nrm((L, EXPERT_FF, D), EXPERT_FF ** -0.5),
        'final_g': gain((D,)),
    }

def reference(x_prompt, x_sample, cache_ckv, cache_krope, c, c_ctx, mod_w, mod_b, norm1_g, w_in,
              q_norm_g, w_uq, kv_norm_g, w_ukv, w_o_attn, conv_w, conv_b, conv_ln_g, conv_ln_b, w_pw2,
              w_out, norm2_g, router_w, router_bias, exp_w_gate, exp_w_up, exp_w_down,
              sh_w_gate, sh_w_up, sh_w_down, final_g):
    def layer_params(l):
        return {
            'norm1_g': norm1_g[l], 'w_in': w_in[l], 'q_norm_g': q_norm_g[l], 'w_uq': w_uq[l],
            'kv_norm_g': kv_norm_g[l], 'w_ukv': w_ukv[l], 'w_o_attn': w_o_attn[l],
            'conv_w': conv_w[l], 'conv_b': conv_b[l], 'conv_ln_g': conv_ln_g[l], 'conv_ln_b': conv_ln_b[l],
            'w_pw2': w_pw2[l], 'w_out': w_out[l], 'norm2_g': norm2_g[l], 'router_w': router_w[l],
            'router_bias': router_bias[l], 'exp_w_gate': exp_w_gate[l], 'exp_w_up': exp_w_up[l],
            'exp_w_down': exp_w_down[l], 'sh_w_gate': sh_w_gate[l], 'sh_w_up': sh_w_up[l],
            'sh_w_down': sh_w_down[l],
        }

    x = x_prompt
    ckv_list, krope_list = [], []
    for l in range(DEPTH):
        mods = adaln(c_ctx[None, :], mod_w[l], mod_b[l])
        x, ckv_l, krope_l = trunk_layer(x, mods, layer_params(l), None, None)
        ckv_list.append(ckv_l)
        krope_list.append(krope_l)
    y_prompt = rmsnorm(x, final_g)
    new_cache_ckv = jnp.stack(ckv_list, axis=1)
    new_cache_krope = jnp.stack(krope_list, axis=1)

    rope = axial_rope(x_sample.shape[1])
    x = x_sample
    for l in range(DEPTH):
        mods = adaln(c, mod_w[l], mod_b[l])
        x, _, _ = trunk_layer(x, mods, layer_params(l), rope, (cache_ckv[:, l], cache_krope[:, l]))
    y_sample = rmsnorm(x, final_g)
    return (y_prompt, y_sample, new_cache_ckv, new_cache_krope)


_drawn_inputs = setup_inputs


def setup_inputs(seed=0):
    import zlib

    import numpy as np

    out = dict(_drawn_inputs(seed))
    spreads = {}
    factors = {'cache_ckv': 3.012,
     'cache_krope': 4.772,
     'q_norm_g': 8.0,
     'conv_b': 4.098,
     'conv_ln_g': 2.872,
     'conv_ln_b': 4.268}
    for name, (base, spread) in spreads.items():
        noise = np.random.default_rng([zlib.crc32(name.encode()), seed]).standard_normal(out[name].shape)
        drawn = base * np.exp(spread * noise) if base else spread * noise
        out[name] = __import__('jax').numpy.asarray(drawn.astype(out[name].dtype))
    for name, factor in factors.items():
        out[name] = (out[name] * factor).astype(out[name].dtype)
    return out
```

```python
from contextlib import ExitStack

import concourse.bass as bass
from concourse import mybir

F32 = mybir.dt.float32
F32R = mybir.dt.float32r
I32 = mybir.dt.int32
ALU = mybir.AluOpType
ACT = mybir.ActivationFunctionType
AX = mybir.AxisListType.X

P = 128
D = 1024
KD = D // P
NT = 3
T = NT * P
TC = P
QL, KVL, RD = 384, 256, 32
H, ND, VD = 16, 64, 64
HD = ND + RD
SCALE = float(HD) ** -0.5
LATW = QL + KVL + RD
CK = 31
PAD = CK // 2
CW = 400
ZW = CW + CK - 1
NE, FF, TOPK, NG = 64, 256, 8, 8
EPS = 1e-6
ROUNDS = T // P
NJ = ROUNDS * NE
BIG = float(1 << 20)
IW = 2048
NRAW, NHL = 4, 3
KB = 256


def constants():
    import numpy as np

    i = np.arange(P)
    parts = {"ident": np.eye(P), "before": (i[:, None] < i[None, :]), "ones": np.ones((P, P)),
             "iota": np.broadcast_to(i[None, :], (P, P))}
    pick = np.zeros((P, 2))
    pick[[2, 3, 4], 0] = 1
    pick[[0, 1, 4], 1] = 1
    parts["pick"] = pick
    parts["pick_rows"] = np.repeat(pick, P, axis=1)
    pos = np.arange(2 * P)
    inv = (np.float32(10000.0) ** (-np.arange(8, dtype=np.float32) / np.float32(8))).astype(np.float32)
    ang = np.stack([(pos // 64).astype(np.float32)[:, None] * inv,
                    (pos % 64).astype(np.float32)[:, None] * inv], axis=1).reshape(2, P, 16)
    parts["cos"] = np.cos(ang).transpose(1, 0, 2).reshape(P, 32)
    parts["sin"] = np.sin(ang).transpose(1, 0, 2).reshape(P, 32)
    parts["token"] = i[:, None] + P * np.arange(NT)[None, :]
    at, n = {}, 0
    for k, v in parts.items():
        at[k] = (n, n + v.shape[1])
        n += v.shape[1]
    return np.concatenate([np.asarray(v, np.float32) for v in parts.values()], axis=1), at


def front_items():
    it = [("mod", b, h) for b in range(4) for h in range(2)]
    it += [("lat", b, h) for b in range(2) for h in range(2)]
    it += [("conv", j) for j in range(KD)]
    it += [("gate", j) for j in range(KD)]
    it += [("uq", b) for b in range(3)]
    it += [("uk",), ("uv",)]
    it += [("mod", b, h) for b in range(4, 12) for h in range(2)]
    it += [("wo", j) for j in range(4)]
    it += [("pw2", j) for j in range(4)]
    it += [("wout", b, h) for b in range(2) for h in range(2)]
    it += [("router",), ("shgu", 0), ("shgu", 1), ("shd",)]
    return it


def psum_groups():
    g = [("vt",), ("cw",)]
    g += [("mod", b) for b in range(4)] + [("modc",)]
    g += [("hT", c) for c in range(KD)]
    g += [("lat", b, t) for b in range(2) for t in range(NT)]
    for j in range(KD):
        g += [("ca", j), ("cg", j)]
        if j == 1:
            g += [("qnT", c) for c in range(3)] + [("ckT", c) for c in range(2)]
    g += [("gl", j) for j in range(16)]
    g += [("uq", b, t) for b in range(3) for t in range(NT)]
    g += [("krT",)]
    g += [("uk", i) for i in range(8)]
    g += [("qT", h) for h in range(H)]
    g += [("uv", kt, b) for kt in range(4) for b in range(2)]
    for h in range(H + 3):
        if h < H:
            g += [("s", h, t) for t in range(NT)]
        if h >= 3 and h % 2 == 1:
            g += [("pv", (h - 3) // 2)]
        if h < H and h % 2 == 0:
            g += [("mod", 4 + h // 2)]
        if 2 <= h < H + 2:
            g += [("pT", h - 2, 0), ("pT", h - 2, 1)]
    g += [("mean",), ("wo", 0), ("wo", 1), ("var",)]
    g += [("wo", j) for j in range(2, KD)]
    g += [("pw2", j) for j in range(KD)]
    g += [("bc", v, c, b) for v in (2, 4, 3) for c in range(2) for b in range(2)]
    g += [("wout", b, t) for b in range(2) for t in range(NT)]
    g += [("bc", 5, c, b) for c in range(2) for b in range(2)]
    g += [("h2T", c) for c in range(KD)]
    g += [("rt", t) for t in range(NT)]
    for t in range(NT):
        g += [("shgu", t)]
    g += [("pos", t) for t in range(NT)] + [("cnt",)]
    for t in range(NT):
        g += [("shT", t)]
    for t in range(NT):
        g += [("shd", t, 0), ("shd", t, 1)]
    return g


def hybrid_step(nc, x_prompt, x_sample, cache_ckv, cache_krope, c, c_ctx, mod_w, mod_b, norm1_g, w_in,
                q_norm_g, w_uq, kv_norm_g, w_ukv, w_o_attn, conv_w, conv_b, conv_ln_g, conv_ln_b, w_pw2,
                w_out, norm2_g, router_w, router_bias, exp_w_gate, exp_w_up, exp_w_down,
                sh_w_gate, sh_w_up, sh_w_down, final_g, consts, at,
                y_prompt, y_sample, new_ckv, new_krope):
    items = front_items()
    item_no = {n: i for i, n in enumerate(items)}
    NI = len(items)
    groups = psum_groups()
    use = {n: (i % 8, i // 8) for i, n in enumerate(groups)}
    assert len(use) == len(groups)

    with ExitStack() as ctx:
        base = 16512

        def sb(name, shape, off_kb, dt=F32):
            return nc.alloc_sbuf_tensor_at(name, shape, dt, offset=base + int(off_kb * 1024))

        def sem(name):
            return ctx.enter_context(nc.semaphore(name))

        def dram(name, shape):
            return nc.dram_tensor(name, shape, F32, kind="Internal").ap()

        psum = [ctx.enter_context(nc.psum_tensor(f"bank{i}", [P, 512], F32)) for i in range(8)]

        raw = [sb(f"raw{i}", [P, IW], 8 * i) for i in range(4)]
        hi = [sb(f"hi{i}", [P, IW], 32 + 8 * i, F32R) for i in range(3)]
        lo = [sb(f"lo{i}", [P, IW], 56 + 8 * i, F32R) for i in range(3)]
        A = 80
        CN = consts.shape[1]
        con = sb("con", [P, CN], A)
        vt = sb("vt", [P, 64], A + 3.625)
        cwt = sb("cwt", [P, KD * CK], A + 3.875)
        stat = sb("stat", [P, 64], A + 5)
        cst = sb("cst", [P, KD * 4], A + 5.25, F32R)
        silc = sb("silc", [P, 16], A + 5.5)
        ab1 = sb("ab1", [P, 32], A + 5.625)
        gkv = sb("gkv", [P, KVL], A + 6)
        rbias = sb("rbias", [P, NE], A + 7)
        mx = sb("mx", [P, 2, 16], A + 7.25)
        rounds_f = sb("rounds_f", [P, 4], A + 7.5)
        rounds_i = sb("rounds_i", [P, 1], A + 7.625, I32)
        kr = sb("kr", [P, 4 * RD], A + 8)
        x = sb("x", [P, NT, D], A + 9)
        modr2 = sb("modr2", [5, 8 * 512], A + 9)
        zb = sb("zb", [P, 9, ZW], A + 25)
        hTh = sb("hTh", [P, KD, T], A + 41, F32R)
        hTl = sb("hTl", [P, KD, T], A + 53, F32R)
        lat = sb("lat", [P, NT + 1, LATW], A + 65)
        sgc = sb("sgc", [P, 2, T], A + 75.5)
        sgs = sb("sgs", [P, 2, T], A + 78.5)
        ftmp = sb("ftmp", [P, 2, T], A + 81.5)
        qnh = sb("qnh", [P, 3, T], A + 84.5, F32R)
        qnl = sb("qnl", [P, 3, T], A + 89, F32R)
        modr1 = sb("modr1", [5, 4 * 512], A + 109)
        xn = sb("xn", [P, NT, D], A + 97)
        junk = sb("junk", [P, D], A + 117)
        vrow = sb("vrow", [P, P], A + 121)
        cwrow = sb("cwrow", [CK, D], A + 121.5)
        ckh = sb("ckh", [P, 2, 512], A + 115.5, F32R)
        ckl = sb("ckl", [P, 2, 512], A + 119.5, F32R)
        qT = sb("qT", [HD, H, T], A + 41)
        kT = sb("kT", [HD, H, 512], A + 65)
        qtok = sb("qtok", [P, NT, H * HD], A + 97)
        rp = sb("rp", [P, 4, 256], A + 123.5)
        V = sb("V", [P, 4, H * VD], A + 97)
        pr = sb("pr", [P, 3, 7 * P], A + 113)
        pT = sb("pT", [P, 7 * P], A + 123.5)
        aT = sb("aT", [P, KD, T], A + 41)
        aTh = sb("aTh", [P, KD, T], A + 65, F32R)
        aTl = sb("aTl", [P, KD, T], A + 77, F32R)
        sigc = sb("sigc", [P, KD, T], A + 89)
        siga = sb("siga", [P, KD, T], A + 53)
        m = sb("m", [P, KD, T], A + 41)
        mt = sb("mt", [P, 2, T], A + 101)
        sq = sb("sq", [P, 2, CW], A + 104)
        lnr = sb("lnr", [P, CW], A + 107.5)
        zf = sb("zf", [P, 2, T], A + 109.25)
        znh = sb("znh", [P, KD, T], A + 25, F32R)
        znl = sb("znl", [P, KD, T], A + 112.5, F32R)
        mh = sb("mh", [P, KD, T], A + 65, F32R)
        ml = sb("ml", [P, KD, T], A + 77, F32R)
        g1 = sb("g1", [P, 2, D], A + 89)
        x1 = sb("x1", [P, NT, D], A + 97)
        xt = sb("xt", [P, 2, 512], A + 109)
        g2row = sb("g2row", [P, D], A + 120)
        a2 = sb("a2", [P, 2, D], A + 25)
        b2 = sb("b2", [P, 2, D], A + 33)
        g2 = sb("g2", [P, 2, D], A + 41)
        h2p = sb("h2p", [P, NT, D], A + 53)
        junk2 = sb("junk2", [P, D], A + 113)
        h2h = sb("h2h", [P, KD, T], A + 81, F32R)
        h2l = sb("h2l", [P, KD, T], A + 109, F32R)
        R = A + 9
        pos3 = sb("pos3", [P, NT, NJ], R)
        vals = sb("vals", [P, NT, NJ, 3], R + 2.25)
        rsc = sb("rsc", [P, NT, NE], R + 9)
        rsel = sb("rsel", [P, NT, NE], R + 9.75)
        rmsk = sb("rmsk", [P, NT, NE], R + 10.5)
        rtmp = sb("rtmp", [P, NT, NE], R + 11.25)
        rrk = sb("rrk", [P, NT, NE], R + 12)
        rg8 = sb("rg8", [P, NT, NG, 8], R + 12.75)
        rgs = sb("rgs", [P, NT, 16], R + 13.5)
        rgr = sb("rgr", [P, NT, 16], R + 13.75)
        rt8 = sb("rt8", [P, NT, 8], R + 14)
        rk8 = sb("rk8", [P, NT, 8], R + 14.125)
        rgm = sb("rgm", [P, NT, 8], R + 14.25)
        rsum = sb("rsum", [P, NT], R + 14.375)
        shs = sb("shs", [P, NT, FF], A + 49)
        shh = sb("shh", [P, NT, FF], A + 52)
        shTh = sb("shTh", [P, NT, FF], A + 55, F32R)
        shTl = sb("shTl", [P, NT, FF], A + 58, F32R)
        shg = sb("shg", [P, 2, 512], A + 61)
        raw += [sb(f"raw{i}", [P, IW], A + 25 + 8 * (i - 4)) for i in (4, 5)]
        hi += [sb(f"hi{i}", [P, IW], A + 41 + 8 * (i - 3), F32R) for i in (3, 4, 5)]
        lo += [sb(f"lo{i}", [P, IW], A + 65 + 8 * (i - 3), F32R) for i in (3, 4, 5)]
        xg = [sb(f"xg{i}", [P, D], A + 89 + 4 * i) for i in range(2)]
        xgh = [sb(f"xgh{i}", [P, KD, P], A + 97 + 4 * i, F32R) for i in range(2)]
        xgl = [sb(f"xgl{i}", [P, KD, P], A + 105 + 4 * i, F32R) for i in range(2)]
        ys = [sb(f"ys{i}", [P, D], A + 113 + 4 * i) for i in range(2)]
        oh = [sb(f"oh{i}", [P, NT, P], A + 121 + 1.5 * i) for i in range(2)]
        sg = sb("sg", [P, FF], R + 9)
        hd = sb("hd", [P, FF], R + 10)
        hdh = [sb(f"hdh{i}", [P, FF], R + 11 + i, F32R) for i in range(2)]
        hdl = [sb(f"hdl{i}", [P, FF], R + 13 + i, F32R) for i in range(2)]
        ixt = [sb(f"ixt{i}", [P, 2], R + 15 + 0.0625 * i, I32) for i in range(4)]
        gsl = [sb(f"gsl{i}", [P, 1], R + 15.25 + 0.0625 * i) for i in range(4)]
        ixs = [sb(f"ixs{i}", [P, 1], R + 15.5 + 0.0625 * i, I32) for i in range(2)]
        slots = [sb(f"slots{i}", [P, TOPK, 512], A + 9 + 16 * i) for i in range(4)]
        tx = [sb(f"tx{i}", [P, D], A + 81 + 4 * i) for i in range(2)]
        tg = sb("tg", [P, 2, D], A + 89)
        tsum = [sb(f"tsum{i}", [P, D], A + 97 + 4 * i) for i in range(2)]
        fgr = sb("fgr", [P, D], A + 105)
        tjunk = sb("tjunk", [P, 512], A + 109)
        tout = [sb(f"tout{i}", [P, D], A + 113 + 4 * i) for i in range(2)]

        sig_d = dram("sig_d", [16, P, T])
        h2_d = dram("h2_d", [T, D])
        x1_d = dram("x1_d", [P, NT, D])
        g2_d = dram("g2_d", [P, 2, D])
        y_d = dram("y_d", [T * TOPK, D])

        def cst_of(name, rows=P):
            a, b = at[name]
            return con[0:rows, a:b]

        ident, before, ones, iota = (cst_of(n) for n in ("ident", "before", "ones", "iota"))
        cosv = cst_of("cos").rearrange("p (t a f) -> p t a f", t=2, a=2)
        sinv = cst_of("sin").rearrange("p (t a f) -> p t a f", t=2, a=2)
        token = cst_of("token")
        V_G1, V_CB, V_LG, V_LB, V_QG, V_C = 0, 8, 16, 24, 32, 35

        small_in = sem("small_in")
        rows_in = sem("rows_in")
        x_in = sem("x_in")
        biasrow1_in, biasrow2_in = sem("biasrow1_in"), sem("biasrow2_in")
        raw_in = [sem(f"raw_in{i}") for i in range(6)]
        hi_done, lo_done, half_used = sem("hi_done"), sem("lo_done"), sem("half_used")
        filled = [sem(f"bank_filled{i}") for i in range(8)]
        act_seq, dve_seq, pool_seq = sem("act_seq"), sem("dve_seq"), sem("pool_seq")
        seq = {"a": 0, "v": 0, "p": 0}
        vt_done, cst_done = sem("vt_done"), sem("cst_done")
        ssq_done, rms_v, rms_a, rstd_done, xn_done = (sem(n) for n in ("ssq_done", "rms_v", "rms_a", "rstd_done", "xn_done"))
        ab1_done, pos_done, var_step, pv_half = sem("ab1_done"), sem("pos_done"), sem("var_step"), sem("pv_half")
        f_done, fhi_done, flo_done = sem("f_done"), sem("fhi_done"), sem("flo_done")
        lat_done, latn_done = sem("lat_done"), sem("latn_done")
        kr_done, krT_done, krep_done = sem("kr_done"), sem("krT_done"), sem("krep_done")
        cks_out = sem("cks_out")
        zpad_done, sgc_done, z_done, conv_step = (sem(n) for n in ("zpad_done", "sgc_done", "z_done", "conv_step"))
        sgs_done, sgs_out = sem("sgs_done"), [sem(f"sgs_out{i}") for i in range(2)]
        qtok_done, qrope_done, qT_act, qT_dve = (sem(n) for n in ("qtok_done", "qrope_done", "qT_act", "qT_dve"))
        kT_done, v_done = sem("kT_done"), sem("v_done")
        nmax_done, exp_done, prn_done = sem("nmax_done"), sem("exp_done"), sem("prn_done")
        pTa_done, pTv_done, pv_out = sem("pTa_done"), sem("pTv_done"), sem("pv_out")
        mod_done = sem("mod_done")
        ahi_done, alo_done = sem("ahi_done"), sem("alo_done")
        siga_in, sigc_in = sem("siga_in"), sem("sigc_in")
        cen_done, sq_done, lnv_done, lns_done, zn_done, zf_done, znh_done, znl_done = (
            sem(n) for n in ("cen_done", "sq_done", "lnv_done", "lns_done", "zn_done", "zf_done", "znh_done", "znl_done"))
        m_done, mh_done, ml_done = sem("m_done"), sem("mh_done"), sem("ml_done")
        xr_in, g2row_in, bc_a, bc_v = sem("xr_in"), sem("g2row_in"), sem("bc_a"), sem("bc_v")
        x1_done, ssq2_done, r2v, r2a, h2_done = (sem(n) for n in ("x1_done", "ssq2_done", "r2v", "r2a", "h2_done"))
        spill_out = sem("spill_out")
        x1_out = sem("x1_out")
        h2d_out = sem("h2d_out")
        h2h_done, h2l_done = sem("h2h_done"), sem("h2l_done")
        rsc_done, mask_done, rtab_done = sem("rsc_done"), sem("mask_done"), sem("rtab_done")
        shs_done, shh_done, shTh_done, shTl_done, shared_added = (
            sem(n) for n in ("shs_done", "shh_done", "shTh_done", "shTl_done", "shared_added"))
        xraw_in = [sem(f"expert_raw_in{i}") for i in range(6)]
        xhi_done, xlo_done = sem("xhi_done"), sem("xlo_done")
        diff_done = sem("diff_done")
        oh_done, list_filled, list_done = sem("oh_done"), sem("list_filled"), sem("list_done")
        ixs_done = sem("ixs_done")
        gathered = [sem(f"gathered{i}") for i in range(2)]
        xgz_done = sem("xgz_done")
        xt_filled, xgh_done, xgl_done = sem("xt_filled"), sem("xgh_done"), sem("xgl_done")
        gu_filled, sg_done, hd_done = sem("gu_filled"), sem("sg_done"), sem("hd_done")
        ht_filled, hdh_done, hdl_done = sem("ht_filled"), sem("hdh_done"), sem("hdl_done")
        dn_filled, ya_done, yv_done = sem("dn_filled"), sem("ya_done"), sem("yv_done")
        scattered = [sem(f"scattered{i}") for i in range(2)]
        slots_in, tx_in, tail_in = [sem(f"slots_in{i}") for i in range(4)], [sem(f"tx_in{i}") for i in range(2)], sem("tail_in")
        tsum_done, t2_done, tss_done, trv, tra, y_done = (
            sem(n) for n in ("tsum_done", "t2_done", "tss_done", "trv", "tra", "y_done"))
        y_out = [sem(f"y_out{i}") for i in range(2)]

        def link(eng, key, ins):
            s = {"a": act_seq, "v": dve_seq, "p": pool_seq}[key]
            seq[key] += 1
            ins.then_inc(s, 1)
            eng.wait_ge(s, seq[key])

        def got(eng, g):
            b, n = use[g]
            eng.wait_ge(filled[b], n + 1)
            return psum[b]

        def read_by(g):
            k = g[0]
            n = g[1] if len(g) > 1 else 0
            return {
                "vt": lambda: (vt_done, 1), "cw": lambda: (vt_done, 2), "mod": lambda: (mod_done, n + 1),
                "modc": lambda: (ab1_done, 3), "hT": lambda: (f_done, n + 1),
                "lat": lambda: (lat_done, NT * n + g[2] + 1),
                "ca": lambda: (z_done, n + 1), "cg": lambda: (sgc_done, n + 1),
                "qnT": lambda: (f_done, KD + n + 1), "ckT": lambda: (flo_done, KD + 3 + n + 1),
                "krT": lambda: (krT_done, 1), "gl": lambda: (sgs_done, n + 1),
                "uq": lambda: (qtok_done, NT * n + g[2] + 1), "uk": lambda: (kT_done, 2 * n + 2),
                "qT": lambda: (qT_dve, (n + 1) // 2) if n % 2 else (qT_act, n // 2 + 1),
                "uv": lambda: (v_done, 2 * n + g[2] + 1), "s": lambda: (exp_done, NT * n + g[2] + 1),
                "pT": lambda: (pTa_done if g[2] else pTv_done, n + 1), "pv": lambda: (pv_out, n + 1),
                "wo": lambda: (m_done, n + 1), "mean": lambda: (cen_done, KD), "var": lambda: (lnv_done, 1),
                "pw2": lambda: (m_done, KD + n + 1),
                "bc": lambda: (bc_v, 2 * g[2] + g[3] + 1) if n == 4 else
                (bc_a, {2: 0, 3: 4, 5: 8}[n] + 2 * g[2] + g[3] + 1),
                "wout": lambda: (x1_done, NT * n + g[2] + 1), "h2T": lambda: (h2l_done, n + 1),
                "rt": lambda: (rsc_done, n + 1), "shgu": lambda: (shh_done, n + 1),
                "pos": lambda: (pos_done, ROUNDS * (n + 1)), "cnt": lambda: (rtab_done, 1),
                "shT": lambda: (shTl_done, n + 1), "shd": lambda: (shared_added, 2 * n + g[2] + 1),
            }[k]()

        halves = [n for n in items if n[0] in ("mod", "lat", "wout", "shgu") and n[-1] == 0]

        def wait_used(eng, i):
            n = items[i]
            if n in halves:
                eng.wait_ge(half_used, halves.index(n) + 1)
                return
            kind, a = n[0], n[1] if len(n) > 1 else 0
            if kind in ("lat", "uq", "wout"):
                last = (kind, a, 2)
            elif kind in ("gate", "wo", "pw2"):
                last = ({"gate": "gl"}.get(kind, kind), 2 * a + 1)
            else:
                last = {"mod": ("mod", a), "conv": ("cg", a), "uk": ("uk", 7), "uv": ("uv", 3, 1),
                        "router": ("rt", 2), "shgu": ("shgu", 2), "shd": ("shd", 2, 1)}[kind]
            got(eng, last)

        LO_GATES = range(item_no[("gate", 0)], item_no[("gate", KD - 1)] + 1)
        LO_MODS = range(item_no[("mod", 5, 0)], item_no[("mod", 11, 1)] + 1)

        def wait_pt_used(eng, h):
            if h % 2:
                got(eng, ("pv", h // 2))
            else:
                eng.wait_ge(pv_half, h // 2 + 1)

        loads = {"conv": 2, "uk": 2, "uv": 2, "shgu": 2}

        def raw_count(i):
            return 16 * sum(loads.get(items[q][0], 1) for q in range(i % NRAW, i + 1, NRAW))

        def uses(i, k):
            return i * 2 + (k // 2 + 1)

        def value(eng, v):
            return v if isinstance(v, int) else eng.to_reg(v)

        def item_shape(n):
            return {"mod": (4, 512), "lat": (4, 336), "conv": (8, 256), "gate": (8, 256), "uq": (3, 512),
                    "uk": (2, 1024), "uv": (2, 1024), "wo": (8, 256), "pw2": (8, 256), "wout": (4, 512),
                    "router": (8, 64), "shgu": (4, 512), "shd": (2, 1024)}[n[0]]

        def cut(tile, n):
            k, w = item_shape(n)
            return tile[:, 0:k * w].rearrange("p (k n) -> p k n", k=k)

        def hl(n):
            i = (item_no[n] - NI) % NHL
            return cut(hi[i], n), cut(lo[i], n)

        def cond_of(t):
            return 0 if t == 0 else 1

        block = ctx.enter_context(nc.Block())

        @block.sync
        def _(sp):
            sp.dma_start(con[:, :], consts).then_inc(rows_in, 16)
            for src, r in ((norm1_g, V_G1), (conv_b, V_CB), (conv_ln_g, V_LG), (conv_ln_b, V_LB),
                           (q_norm_g, V_QG)):
                n = src.shape[-1] // P
                sp.dma_start(vrow[r:r + n, :], src[0].rearrange("(a b) -> a b", b=P)).then_inc(rows_in, 16)
            sp.dma_start(vrow[V_C:V_C + 8, :], c[0].rearrange("(a b) -> a b", b=P)).then_inc(rows_in, 16)
            sp.dma_start(vrow[V_C + 8:V_C + 16, :], c_ctx.rearrange("(a b) -> a b", b=P)).then_inc(rows_in, 16)
            sp.dma_start(cwrow[:, :], conv_w[0]).then_inc(rows_in, 16)
            sp.dma_start(modr1[4:5, :], mod_b[:, 0:2048]).then_inc(biasrow1_in, 16)

            def src_of(n):
                kind = n[0]
                if kind == "mod":
                    _, b, h = n
                    return mod_w[0, 512 * h:512 * h + 512, 512 * b:512 * b + 512]
                if kind == "lat":
                    _, b, h = n
                    return w_in[0, 512 * h:512 * h + 512, 336 * b:336 * b + 336]
                if kind == "gate":
                    return w_in[0, :, LATW + 2048 + 256 * n[1]:LATW + 2048 + 256 * n[1] + 256]
                if kind == "uq":
                    return w_uq[0, :, 512 * n[1]:512 * n[1] + 512]
                if kind in ("wo", "pw2"):
                    return {"wo": w_o_attn, "pw2": w_pw2}[kind][0, :, 256 * n[1]:256 * n[1] + 256]
                if kind == "wout":
                    _, b, h = n
                    return w_out[0, 512 * h:512 * h + 512, 512 * b:512 * b + 512]
                return None

            def load(i):
                n = items[i]
                s = (i - NI) % NRAW
                if i >= NRAW:
                    sp.wait_ge(lo_done, i - NRAW + 1)
                dst = cut(raw[s], n)
                src = src_of(n)
                if src is not None:
                    sp.dma_start(dst, src.rearrange("(k p) n -> p k n", p=P)).then_inc(raw_in[s], 16)
                elif n[0] == "conv":
                    j = n[1]
                    for half in range(2):
                        a = LATW + 1024 * half + P * j
                        sp.dma_start(dst[:, :, P * half:P * half + P],
                                     w_in[0, :, a:a + P].rearrange("(k p) n -> p k n", p=P)).then_inc(raw_in[s], 16)
                elif n[0] in ("uk", "uv"):
                    o = 0 if n[0] == "uk" else ND
                    w = w_ukv[0].rearrange("(k p) (h n) -> p k h n", p=P, h=H)
                    for k in range(2):
                        sp.dma_start(dst[:, k, :].rearrange("p (h n) -> p h n", h=H),
                                     w[:, k, :, o:o + ND]).then_inc(raw_in[s], 16)
                elif n[0] == "router":
                    sp.dma_start(dst, router_w[0].rearrange("(p k) n -> p k n", k=KD)).then_inc(raw_in[s], 16)
                elif n[0] == "shgu":
                    for w, src2 in enumerate((sh_w_gate, sh_w_up)):
                        v = src2[0].rearrange("(p k) n -> p k n", k=KD)[:, 4 * n[1]:4 * n[1] + 4, :]
                        sp.dma_start(dst[:, :, FF * w:FF * w + FF], v).then_inc(raw_in[s], 16)
                elif n[0] == "shd":
                    sp.dma_start(dst, sh_w_down[0].rearrange("(p k) n -> p k n", k=2)).then_inc(raw_in[s], 16)

            for i in range(4):
                load(i)
            sp.dma_start(x[:, 0, :], x_prompt[0]).then_inc(x_in, 16)
            sp.dma_start(x[:, 1:3, :], x_sample[0].rearrange("(t p) d -> p t d", p=P)).then_inc(x_in, 16)
            sp.dma_start(gkv[:, :], kv_norm_g.partition_broadcast(P)).then_inc(small_in, 16)
            sp.dma_start(rbias[:, :], router_bias.partition_broadcast(P)).then_inc(small_in, 16)
            sp.dma_start(lat[:, 3, QL:QL + KVL], cache_ckv[0, 0]).then_inc(small_in, 16)
            sp.dma_start(kr[:, 3 * RD:4 * RD], cache_krope[0, 0]).then_inc(small_in, 16)
            for i in range(4, NI):
                load(i)
                if items[i] == ("wo", 3):
                    sp.wait_ge(sgs_out[0], 16 * 8)
                    sp.wait_ge(sgs_out[1], 16 * 8)
                    sp.wait_ge(pv_out, KD)
                    sp.dma_start(siga[:, :, :], sig_d[0:8].rearrange("j p t -> p j t")).then_inc(siga_in, 16)
                    sp.dma_start(sigc[:, :, :], sig_d[8:16].rearrange("j p t -> p j t")).then_inc(sigc_in, 16)
                if items[i] == ("wout", 0, 1):
                    sp.wait_ge(pv_out, KD)
                    sp.wait_ge(m_done, 2 * KD)
                    sp.wait_ge(ml_done, KD)
                    sp.dma_start(x1[:, 0, :], x_prompt[0]).then_inc(xr_in, 16)
                    sp.dma_start(x1[:, 1:3, :], x_sample[0].rearrange("(t p) d -> p t d", p=P)).then_inc(xr_in, 16)
                    got(sp, ("pw2", 7))
                    sp.dma_start(g2row[:, :], norm2_g.partition_broadcast(P)).then_inc(g2row_in, 16)

            def load_expert(i, k):
                j = i * 4 + k
                e = j % NE
                one = slice(e, e + 1) if isinstance(e, int) else bass.ds(e, 1)
                for q in range(3):
                    s = 3 * (k % 2) + q
                    if isinstance(j, int) and j == 0:
                        sp.wait_ge(lo_done, NI - 3 + q)
                    if not isinstance(j, int) or j >= 2:
                        sp.wait_ge(xlo_done, 3 * (j - 2) + (q + 1))
                    if q < 2:
                        v = raw[s][:, :].rearrange("p (w n) -> p w n", w=2)
                        for w, src in enumerate((exp_w_gate, exp_w_up)):
                            sv = src[0, one].rearrange("a (p k) n -> (a p) (k n)", k=KD)
                            sp.dma_start(v[:, w, :], sv[:, 1024 * q:1024 * q + 1024]).then_inc(xraw_in[s], 16)
                    else:
                        sv = exp_w_down[0, one].rearrange("a (p k) n -> (a p) (k n)", k=2)
                        sp.dma_start(raw[s][:, :], sv).then_inc(xraw_in[s], 16)

            load_expert(0, 0)
            sp.wait_ge(lo_done, NI)
            sp.wait_ge(h2_done, NT)
            load_expert(0, 1)
            for k in (2, 3):
                load_expert(0, k)
            sp.wait_ge(rtab_done, 1)
            last = sp.value_load(rounds_i[0:1, 0:1], min_val=NE // 4 - 2, max_val=ROUNDS * NE // 4 - 2) + 1
            with sp.Fori(1, last + 1) as i:
                for k in range(4):
                    load_expert(i, k)

            N = value(sp, last * 4 + 4)
            sent = value(sp, (last * 4 + 4) * 8)
            sp.wait_ge(rtab_done, 1)
            sp.wait_ge(dn_filled, N)
            sp.wait_ge(ya_done, N)
            sp.wait_ge(yv_done, N)
            for u in range(2):
                sp.wait_ge(scattered[u], sent)
            rows = y_d.rearrange("(t k) d -> t k d", k=TOPK)
            for n in range(2 * NT):
                t, b = n // 2, n % 2
                if n >= 4:
                    sp.wait_ge(tsum_done, n - 3)
                sp.dma_start(slots[n % 4][:, :, :],
                             rows[t * P:(t + 1) * P, :, 512 * b:512 * b + 512]).then_inc(slots_in[n % 4], 16)
                if n == 0:
                    sp.dma_start(tg[:, :, :], g2_d).then_inc(tail_in, 16)
                    sp.dma_start(fgr[:, :], final_g.rearrange("(a n) -> a n", a=1).partition_broadcast(P)).then_inc(tail_in, 16)
                if b == 0:
                    if t >= 2:
                        sp.wait_ge(t2_done, 2 * (t - 1))
                    sp.dma_start(tx[t % 2][:, :], x1_d[:, t, :]).then_inc(tx_in[t % 2], 16)
            for t in range(NT):
                sp.wait_ge(y_done, t + 1)
                dst = y_prompt[0] if t == 0 else y_sample[0, (t - 1) * P:t * P, :]
                sp.dma_start(dst, tout[t % 2][:, :]).then_inc(y_out[t % 2], 16)
            for u in range(2):
                sp.wait_ge(y_out[u], 16 * ((NT + 1 - u) // 2))
            sp.wait_ge(cks_out, 32)

        @block.gpsimd
        def _(pool):
            pool.memset(zb[:, :, :], 0.0).then_inc(zpad_done, 1)
            pool.wait_ge(latn_done, 2 * NT)
            pool.dma_start(new_ckv[0, 0], lat[:, 0, QL:QL + KVL]).then_inc(cks_out, 16)
            pool.dma_start(new_krope[0, 0], lat[:, 0, QL + KVL:LATW]).then_inc(cks_out, 16)

            def split(i):
                pool.wait_ge(hi_done, i + 1)
                pool.wait_ge(lo_done, i)
                pool.tensor_tensor(lo[(i - NI) % NHL][:, :], raw[(i - NI) % NRAW][:, :],
                                   hi[(i - NI) % NHL][:, :].bitcast(F32), ALU.subtract).then_inc(lo_done, 1)

            for i in LO_GATES:
                split(i)
            pool.wait_ge(krT_done, 1)
            pool.tensor_copy(kT[ND:HD, 1:H, :], kT[ND:HD, 0:1, :].to_broadcast([RD, H - 1, 512])).then_inc(krep_done, 1)
            pool.wait_ge(xn_done, NT)
            pool.dma_start(modr2[4:5, :], mod_b[:, 2048:6144]).then_inc(biasrow2_in, 16)
            for i in LO_MODS:
                split(i)
            pool.wait_ge(bc_a, 12)
            pool.dma_start(g2_d, g2[:, :, :]).then_inc(spill_out, 16)
            for t in range(NT):
                pool.wait_ge(h2_done, t + 1)
                pool.dma_start(h2_d[t * P:(t + 1) * P, :], h2p[:, t, :]).then_inc(h2d_out, 16)
            pool.wait_ge(rtab_done, 1)
            last = pool.value_load(rounds_i[0:1, 0:1], min_val=NE // 4 - 2, max_val=ROUNDS * NE // 4 - 2) + 1

            def onehot(i, k):
                j = i * 4 + k
                if not isinstance(j, int) or j >= 2:
                    pool.wait_ge(list_filled, j - 1)
                one = slice(j, j + 1) if isinstance(j, int) else bass.ds(j, 1)
                subtracted = value(pool, j + 1)
                pool.tensor_tensor(oh[k % 2][:, :, :], iota.unsqueeze(1).to_broadcast([P, NT, P]),
                                   pos3[:, :, one].to_broadcast([P, NT, P]), ALU.subtract).then_inc(diff_done, 1)
                pool.wait_ge(rtab_done, 1)
                pool.wait_ge(diff_done, subtracted)
                pool.tensor_scalar(oh[k % 2][:, :, :], oh[k % 2][:, :, :], 0.0, None, ALU.is_equal).then_inc(oh_done, 1)

            def gather(i, k):
                j = i * 4 + k
                listed, turned = value(pool, j + 1), value(pool, j - 1)
                pool.wait_ge(rtab_done, 1)
                pool.wait_ge(list_done, listed)
                if not isinstance(j, int) or j >= 2:
                    pool.wait_ge(xt_filled, turned)
                pool.indirect_dma_start(xg[k % 2][:, :], None, h2_d,
                                        bass.IndirectOffsetOnAxis(ap=ixt[k % 4][:, 0:1], axis=0),
                                        bounds_check=T - 1, oob_is_err=False).then_inc(gathered[k % 2], 16)

            def scatter_rows(i, k):
                j = i * 4 + k
                listed, sent = value(pool, j + 1), value(pool, uses(i, k - 2) * 16)
                pool.wait_ge(rtab_done, 1)
                pool.wait_ge(list_done, listed)
                if not isinstance(j, int) or j >= 2:
                    pool.wait_ge(scattered[k % 2], sent)
                pool.tensor_copy(ixs[k % 2][:, :], ixt[k % 4][:, 1:2]).then_inc(ixs_done, 1)

            def scatter(i, k):
                j = i * 4 + k
                filled = value(pool, j + 1)
                pool.wait_ge(rtab_done, 1)
                pool.wait_ge(ya_done, filled)
                pool.wait_ge(yv_done, filled)
                pool.wait_ge(ixs_done, filled)
                pool.indirect_dma_start(y_d, bass.IndirectOffsetOnAxis(ap=ixs[k % 2][:, 0:1], axis=0),
                                        ys[k % 2][:, :], None,
                                        bounds_check=TOPK * T - 1, oob_is_err=False).then_inc(scattered[k % 2], 16)

            def step(i, k, left=9):
                if left > 2:
                    gather(i, k + 2)
                if not isinstance(i, int) or 4 * i + k > 0:
                    scatter_rows(i, k - 1)
                if left > 3:
                    onehot(i, k + 3)
                if not isinstance(i, int) or 4 * i + k > 0:
                    scatter(i, k - 1)

            pool.wait_ge(pos_done, ROUNDS * NT)
            onehot(0, 0)
            onehot(0, 1)
            got(pool, ("shgu", 2))
            for u in range(2):
                pool.memset(xg[u][:, :], 0.0).then_inc(xgz_done, 1)
            pool.wait_ge(xgz_done, 2)
            pool.wait_ge(h2d_out, 16 * NT)
            gather(0, 0)
            onehot(0, 2)
            gather(0, 1)
            for k in range(4):
                step(0, k)
            with pool.Fori(1, last) as i:
                for k in range(4):
                    step(i, k)
            for k in range(4):
                step(last, k, left=4 - k)
            scatter_rows(last, 3)
            scatter(last, 3)

        @block.scalar
        def _(act):
            def split(i):
                if i >= NI:
                    return
                n = items[i]
                act.wait_ge(raw_in[(i - NI) % NRAW], raw_count(i))
                if i >= NHL:
                    wait_used(act, i - NHL)
                k, w = item_shape(n)
                act.activation(hi[(i - NI) % NHL][:, 0:k * w], raw[(i - NI) % NRAW][:, 0:k * w], ACT.Copy).then_inc(hi_done, 1)

            p = got(act, ("vt",))
            act.activation(vt[:, 0:51], p[:, 0:51], ACT.Copy).then_inc(vt_done, 1)
            act.wait_ge(vt_done, 1)
            link(act, "a", act.activation(silc[:, :], vt[:, V_C:V_C + 16], ACT.Silu))
            for cc in range(2):
                ins = act.activation(cst[:, :].rearrange("p (k r) -> p k r", r=4)[:, :, 2 * cc],
                                     silc[:, 8 * cc:8 * cc + 8], ACT.Copy)
                ins.then_inc(cst_done, 1)
            p = got(act, ("cw",))
            act.activation(cwt[:, :], p[:, 0:KD * CK], ACT.Copy).then_inc(vt_done, 1)
            split(0)
            split(1)

            def mod_rows(b, dst):
                g = ("mod", b)
                p = got(act, g)
                act.activation(dst, p[0:4, :], ACT.Copy).then_inc(mod_done, 1)

            for b in range(4):
                split(item_no[("mod", b, 0)] + 2)
                split(item_no[("mod", b, 1)] + 2)
                mod_rows(b, modr1[0:4, 512 * b:512 * b + 512])
                if b == 0:
                    act.wait_ge(x_in, 32)
                    for t in range(NT):
                        if t:
                            act.wait_ge(ssq_done, t)
                        act.activation(junk[:, :], x[:, t, :], ACT.Square,
                                       accum_out=stat[:, t:t + 1]).then_inc(ssq_done, 1)
                if b == 1:
                    act.wait_ge(rms_v, 1)
                    act.activation(stat[:, 8:11], stat[:, 4:7], ACT.Sqrt).then_inc(rms_a, 1)
            for c8 in range(KD):
                act.wait_ge(f_done, c8 + 1)
                act.activation(hTh[:, c8, :], ftmp[:, c8 % 2, :], ACT.Copy).then_inc(fhi_done, 1)
            for b in range(2):
                split(item_no[("lat", b, 0)] + 2)
                split(item_no[("lat", b, 1)] + 2)
                for t in range(NT):
                    p = got(act, ("lat", b, t))
                    act.activation(lat[:, t, 336 * b:336 * b + 336], p[:, 0:336], ACT.Copy).then_inc(lat_done, 1)
            act.wait_ge(lat_done, 2 * NT)
            for t in range(NT):
                act.activation(junk[:, 0:QL], lat[:, t, 0:QL], ACT.Square, accum_out=stat[:, 16 + t:17 + t]).then_inc(ssq_done, 1)
                act.wait_ge(ssq_done, NT + 2 * t + 1)
                act.activation(junk[:, 0:KVL], lat[:, t, QL:QL + KVL], ACT.Square, accum_out=stat[:, 19 + t:20 + t]).then_inc(ssq_done, 1)
                act.wait_ge(ssq_done, NT + 2 * t + 2)
            act.wait_ge(rms_v, 2)
            act.activation(stat[:, 32:38], stat[:, 24:30], ACT.Sqrt).then_inc(rms_a, 1)

            for j in range(KD):
                split(item_no[("conv", j)] + 2)
                p = got(act, ("cg", j))
                if j >= 2:
                    act.wait_ge(z_done, j - 1)
                act.activation(sgc[:, j % 2, :], p[:, 0:T], ACT.Sigmoid).then_inc(sgc_done, 1)
                if j == 1:
                    for k in range(3):
                        act.wait_ge(f_done, KD + k + 1)
                        act.activation(qnh[:, k, :], ftmp[:, k % 2, :], ACT.Copy).then_inc(fhi_done, 1)
                    for k in range(2):
                        p = got(act, ("ckT", k))
                        act.activation(ckh[:, k, :], p[:, :], ACT.Copy).then_inc(fhi_done, 1)

            def spill_gate(j):
                act.wait_ge(sgs_done, j + 1)
                act.dma_start(sig_d[j], sgs[:, j % 2, :]).then_inc(sgs_out[j % 2], 16)

            for j in range(16):
                if j % 2 == 0:
                    split(item_no[("gate", j // 2)] + 2)
                p = got(act, ("gl", j))
                if j >= 2:
                    act.wait_ge(sgs_out[j % 2], 16 * (j // 2))
                act.activation(sgs[:, j % 2, :], p[:, 0:T], ACT.Sigmoid).then_inc(sgs_done, 1)
                if j:
                    spill_gate(j - 1)
            spill_gate(15)
            for b in range(3):
                split(item_no[("uq", b)] + 2)
                for t in range(NT):
                    p = got(act, ("uq", b, t))
                    act.activation(qtok[:, t, 512 * b:512 * b + 512], p[:, :], ACT.Copy).then_inc(qtok_done, 1)
            split(item_no[("uk",)] + 2)
            got(act, ("uq", 2, 2))
            act.wait_ge(cks_out, 32)
            act.wait_ge(sgs_out[0], 16 * 8)
            act.wait_ge(sgs_out[1], 16 * 8)
            p = got(act, ("krT",))
            act.activation(kT[ND:HD, 0, :], p[0:RD, :], ACT.Copy).then_inc(krT_done, 1)
            for i in range(8):
                p = got(act, ("uk", i))
                act.activation(kT[0:ND, 2 * i, :], p[0:ND, :], ACT.Copy).then_inc(kT_done, 1)
                act.activation(kT[0:ND, 2 * i + 1, :], p[ND:P, :], ACT.Copy).then_inc(kT_done, 1)
            for h in range(0, H, 2):
                p = got(act, ("qT", h))
                act.activation(qT[:, h, :], p[0:HD, 0:T], ACT.Copy).then_inc(qT_act, 1)
            split(item_no[("uv",)] + 2)
            for kt in range(4):
                for b in range(2):
                    p = got(act, ("uv", kt, b))
                    act.activation(V[:, kt, 512 * b:512 * b + 512], p[:, :], ACT.Copy).then_inc(v_done, 1)

            def exps(h):
                for t in range(NT):
                    a, w = (0, P) if t == 0 else (P + 384 * (t - 1), 384)
                    act.wait_ge(nmax_done, NT * h + t + 1)
                    if t == 0 and h >= 3:
                        got(act, ("pT", h - 3, 1))
                    p = got(act, ("s", h, t))
                    act.activation(pr[:, h % 3, a:a + w], p[:, 0:w], ACT.Exp, scale=SCALE,
                                   bias=mx[:, h % 2, t:t + 1],
                                   accum_out=mx[:, h % 2, 4 + t:5 + t]).then_inc(exp_done, 1)

            for h in range(H + 4):
                if h < H:
                    exps(h)
                if h >= 4 and h % 2 == 0:
                    i = (h - 4) // 2
                    p = got(act, ("pv", i))
                    act.activation(aT[:, i, :], p[:, 0:T], ACT.Copy).then_inc(pv_out, 1)
                if h < H:
                    b = 4 + h // 2
                    split(item_no[("mod", b, h % 2)] + 2)
                    if h % 2 == 1:
                        mod_rows(b, modr2[0:4, 512 * (b - 4):512 * (b - 4) + 512])
                if 2 <= h < H + 2:
                    p = got(act, ("pT", h - 2, 0))
                    if h >= 3:
                        wait_pt_used(act, h - 3)
                    act.activation(pT[:, 0:512], p[:, :], ACT.Copy).then_inc(pTv_done, 1)
                    p = got(act, ("pT", h - 2, 1))
                    act.activation(pT[:, 512:896], p[:, 0:384], ACT.Copy).then_inc(pTa_done, 1)
            act.wait_ge(pv_out, KD)
            for k in range(KD):
                act.activation(aTh[:, k, :], aT[:, k, :], ACT.Copy).then_inc(ahi_done, 1)
            split(item_no[("wo", 0)] + 2)
            for k in range(KD):
                act.wait_ge(cen_done, k + 1)
                if k >= 2:
                    act.wait_ge(var_step, k - 1)
                act.activation(sq[:, k % 2, :], zb[:, k, 0:CW], ACT.Square).then_inc(sq_done, 1)
            split(item_no[("wo", 1)] + 2)
            act.wait_ge(lnv_done, 1)
            act.activation(sq[:, 1, :], sq[:, 0, :], ACT.Sqrt).then_inc(lns_done, 1)
            for k in range(KD):
                act.wait_ge(zn_done, k + 1)
                if k >= 2:
                    act.wait_ge(znl_done, k - 1)
                for a, b, o in ((0, P, 0), (P + PAD, P + PAD + 2 * P, P)):
                    act.activation(zf[:, k % 2, o:o + b - a], zb[:, k, a:b], ACT.Silu,
                                   scale=vt[:, V_LG + k:V_LG + k + 1], bias=vt[:, V_LB + k:V_LB + k + 1]).then_inc(zf_done, 1)
                act.wait_ge(zf_done, 2 * k + 2)
                act.activation(znh[:, k, :], zf[:, k % 2, :], ACT.Copy).then_inc(znh_done, 1)
            for j in (2, 3):
                split(item_no[("wo", j)] + 2)
            for j in range(4):
                split(item_no[("pw2", j)] + 2)
                for k in (2 * j, 2 * j + 1):
                    act.wait_ge(m_done, KD + k + 1)
                    act.activation(mh[:, k, :], m[:, k, :], ACT.Copy).then_inc(mh_done, 1)

            def rows_of(v, dst):
                for cc in range(2):
                    for b in range(2):
                        p = got(act, ("bc", v, cc, b))
                        act.activation(dst[:, cc, 512 * b:512 * b + 512], p[:, :], ACT.Copy).then_inc(bc_a, 1)

            rows_of(2, g1)
            rows_of(3, b2)
            for b in range(2):
                split(item_no[("wout", b, 0)] + 2)
                split(item_no[("wout", b, 1)] + 2)
            for t in range(NT):
                act.wait_ge(x1_done, NT + t + 1)
                if t:
                    act.wait_ge(ssq2_done, t)
                act.activation(junk2[:, :], x1[:, t, :], ACT.Square, accum_out=stat[:, 40 + t:41 + t]).then_inc(ssq2_done, 1)
                act.wait_ge(r2v, t + 1)
                act.activation(stat[:, 48 + t:49 + t], stat[:, 44 + t:45 + t], ACT.Sqrt).then_inc(r2a, 1)
            rows_of(5, g2)
            for k in range(KD):
                p = got(act, ("h2T", k))
                act.activation(h2h[:, k, :], p[:, 0:T], ACT.Copy).then_inc(h2h_done, 1)
            split(item_no[("router",)] + 2)
            for t in range(NT):
                p = got(act, ("rt", t))
                act.activation(rsc[:, t, :], p[:, 0:NE], ACT.Sigmoid).then_inc(rsc_done, 1)
            split(item_no[("shgu", 0)] + 2)
            act.wait_ge(h2d_out, 16 * NT)
            for t in range(NT):
                p = got(act, ("shgu", t))
                act.activation(shs[:, t, :], p[:, 0:FF], ACT.Silu).then_inc(shs_done, 1)
            def xsplit(i, k, q):
                j, s = i * 4 + k, 3 * (k % 2) + q
                act.wait_ge(xraw_in[s], uses(i, k) * (32 if q < 2 else 16))
                if not isinstance(j, int) or j >= 2:
                    act.wait_ge(gu_filled if q < 2 else dn_filled, j - 1)
                if q < 2:
                    src = raw[s][:, :].rearrange("p (w k n) -> p k w n", w=2, k=4)
                    dst = hi[s][:, :].rearrange("p (k w n) -> p k w n", w=2, k=4)
                else:
                    src, dst = raw[s][:, :], hi[s][:, :]
                act.activation(dst, src, ACT.Copy).then_inc(xhi_done, 1)

            xsplit(0, 0, 0)
            xsplit(0, 0, 1)
            for t in range(NT):
                p = got(act, ("shT", t))
                act.activation(shTh[:, t, :], p[:, 0:FF], ACT.Copy).then_inc(shTh_done, 1)
            act.wait_ge(shared_added, 2 * NT)
            act.dma_start(x1_d, x1[:, :, :]).then_inc(x1_out, 16)

            act.wait_ge(rtab_done, 1)
            last = act.value_load(rounds_i[0:1, 0:1], min_val=NE // 4 - 2, max_val=ROUNDS * NE // 4 - 2) + 1

            def turn_hi(i, k):
                j = i * 4 + k
                act.wait_ge(xt_filled, j + 1)
                if not isinstance(j, int) or j >= 2:
                    act.wait_ge(gu_filled, j - 1)
                for b in range(2):
                    act.activation(xgh[k % 2][:, 4 * b:4 * b + 4, :],
                                   psum[2 + b][:, :].rearrange("p (k n) -> p k n", k=4), ACT.Copy).then_inc(xgh_done, 1)

            def rows_out(i, k):
                j = i * 4 + k
                act.wait_ge(dn_filled, j + 1)
                if not isinstance(j, int) or j >= 2:
                    act.wait_ge(scattered[k % 2], uses(i, k - 2) * 16)
                act.activation(ys[k % 2][:, 0:512], psum[6][:, :], ACT.Copy).then_inc(ya_done, 1)

            def step(i, k, left=9):
                j = i * 4 + k
                early = isinstance(j, int) and j < 1
                if left > 1:
                    turn_hi(i, k + 1)
                    xsplit(i, k + 1, 0)
                    xsplit(i, k + 1, 1)
                act.wait_ge(gu_filled, j + 1)
                if not early:
                    act.wait_ge(hd_done, j)
                act.activation(sg[:, :], psum[k % 2][:, 0:FF], ACT.Silu).then_inc(sg_done, 1)
                if left > 1:
                    xsplit(i, k + 1, 2)
                if not early:
                    rows_out(i, k - 1)
                act.wait_ge(ht_filled, j + 1)
                act.activation(hdh[k % 2][:, :], psum[4][:, 0:FF], ACT.Copy).then_inc(hdh_done, 1)

            xsplit(0, 0, 2)
            act.wait_ge(spill_out, 16)
            act.wait_ge(x1_out, 16)
            turn_hi(0, 0)
            for k in range(4):
                step(0, k)
            with act.Fori(1, last) as i:
                for k in range(4):
                    step(i, k)
            for k in range(4):
                step(last, k, left=4 - k)
            rows_out(last, 3)

            for t in range(NT):
                for b in range(2):
                    n = 2 * t + b
                    act.wait_ge(t2_done, n + 1)
                    if n:
                        act.wait_ge(tss_done, n)
                    act.activation(tjunk[:, :], tsum[t % 2][:, 512 * b:512 * b + 512], ACT.Square,
                                   accum_out=stat[:, 16 + n:17 + n]).then_inc(tss_done, 1)
                act.wait_ge(trv, t + 1)
                act.activation(stat[:, 60 + t:61 + t], stat[:, 57 + t:58 + t], ACT.Sqrt).then_inc(tra, 1)

        @block.vector
        def _(dve):
            def split(i):
                if i >= NI:
                    return
                if i in LO_GATES or i in LO_MODS:
                    return
                if i - 1 in LO_GATES or i - 1 in LO_MODS:
                    dve.wait_ge(lo_done, i)
                n = items[i]
                dve.wait_ge(hi_done, i + 1)
                k, w = item_shape(n)
                dve.tensor_tensor(lo[(i - NI) % NHL][:, 0:k * w], raw[(i - NI) % NRAW][:, 0:k * w],
                                  hi[(i - NI) % NHL][:, 0:k * w].bitcast(F32), ALU.subtract).then_inc(lo_done, 1)

            dve.wait_ge(cst_done, 2)
            for cc in range(2):
                dve.tensor_tensor(cst[:, :].rearrange("p (k r) -> p k r", r=4)[:, :, 2 * cc + 1],
                                  silc[:, 8 * cc:8 * cc + 8],
                                  cst[:, :].rearrange("p (k r) -> p k r", r=4)[:, :, 2 * cc].bitcast(F32),
                                  ALU.subtract).then_inc(cst_done, 1)
            split(0)
            split(1)
            for i in range(8):
                split(i + 2)
                if i == 1:
                    dve.wait_ge(ssq_done, NT)
                    dve.tensor_scalar(stat[:, 4:7], stat[:, 0:3], 1.0 / D, EPS, ALU.mult, ALU.add).then_inc(rms_v, 1)
                if i == 3:
                    dve.wait_ge(rms_a, 1)
                    dve.reciprocal(stat[:, 12:15], stat[:, 8:11]).then_inc(rstd_done, 1)
                    dve.wait_ge(rstd_done, 1)
                    for t in range(NT):
                        dve.tensor_scalar(xn[:, t, :], x[:, t, :], stat[:, 12 + t:13 + t], None, ALU.mult).then_inc(xn_done, 1)
            p = got(dve, ("modc",))
            pv = p[:, 0:32].rearrange("p (v k c) -> p v c k", v=2, c=2)
            abv = ab1[:, :].rearrange("p (v c k) -> p v c k", v=2, c=2)
            for cc in range(2):
                dve.scalar_tensor_tensor(out=abv[:, 0, cc, :], in0=pv[:, 1, cc, :], scalar=1.0,
                                         in1=vt[:, V_G1:V_G1 + 8], op0=ALU.add, op1=ALU.mult).then_inc(ab1_done, 1)
            dve.tensor_copy(abv[:, 1, :, :], pv[:, 0, :, :]).then_inc(ab1_done, 1)
            dve.wait_ge(ab1_done, 3)
            for k in range(KD):
                p = got(dve, ("hT", k))
                if k >= 2:
                    dve.wait_ge(flo_done, k - 1)
                for cc, a, b in ((0, 0, TC), (1, TC, T)):
                    ins = dve.tensor_scalar(ftmp[:, k % 2, a:b], p[:, a:b], abv[:, 0, cc, k:k + 1],
                                            abv[:, 1, cc, k:k + 1], ALU.mult, ALU.add)
                ins.then_inc(f_done, 1)
                if k:
                    dve.wait_ge(fhi_done, k)
                    dve.tensor_tensor(hTl[:, k - 1, :], ftmp[:, (k - 1) % 2, :], hTh[:, k - 1, :].bitcast(F32),
                                      ALU.subtract).then_inc(flo_done, 1)
            dve.wait_ge(fhi_done, KD)
            dve.tensor_tensor(hTl[:, KD - 1, :], ftmp[:, (KD - 1) % 2, :], hTh[:, KD - 1, :].bitcast(F32),
                              ALU.subtract).then_inc(flo_done, 1)
            for b in range(2):
                split(item_no[("lat", b, 0)] + 2)
                split(item_no[("lat", b, 1)] + 2)
            dve.wait_ge(small_in, 64)
            dve.wait_ge(ssq_done, 3 * NT)
            link(dve, "v", dve.tensor_scalar(stat[:, 24:27], stat[:, 16:19], 1.0 / QL, EPS, ALU.mult, ALU.add))
            dve.tensor_scalar(stat[:, 27:30], stat[:, 19:22], 1.0 / KVL, EPS, ALU.mult, ALU.add).then_inc(rms_v, 1)
            dve.wait_ge(rms_a, 2)
            dve.reciprocal(stat[:, 32:38], stat[:, 32:38]).then_inc(rstd_done, 1)
            dve.wait_ge(rstd_done, 2)
            for t in range(NT):
                dve.tensor_scalar(lat[:, t, 0:QL], lat[:, t, 0:QL], stat[:, 32 + t:33 + t], None, ALU.mult).then_inc(latn_done, 1)
                dve.scalar_tensor_tensor(out=lat[:, t, QL:QL + KVL], in0=lat[:, t, QL:QL + KVL],
                                         scalar=stat[:, 35 + t:36 + t], in1=gkv[:, :],
                                         op0=ALU.mult, op1=ALU.mult).then_inc(latn_done, 1)

            def rope(dst, src, tt, nh):
                cs = cosv[:, tt].unsqueeze(1).to_broadcast([P, nh, 2, 8])
                sn = sinv[:, tt].unsqueeze(1).to_broadcast([P, nh, 2, 8])
                w = nh * 16
                v = [rp[:, q, 0:w].rearrange("p (h a f) -> p h a f", h=nh, a=2) for q in range(4)]
                a, b = src[:, :, :, 0, :], src[:, :, :, 1, :]
                for q, (s, tr) in enumerate(((a, cs), (b, sn), (a, sn), (b, cs))):
                    ins = dve.tensor_tensor(v[q], s, tr, ALU.mult)
                    if q == 3:
                        link(dve, "v", ins)
                dve.tensor_tensor(dst[:, :, :, 0, :], v[0], v[1], ALU.subtract)
                link(dve, "v", dve.tensor_tensor(dst[:, :, :, 1, :], v[2], v[3], ALU.add))

            def head_view(ap, nh):
                return ap.rearrange("p (h a b f) -> p h a b f", h=nh, a=2, b=2)

            for t in (1, 2):
                rope(head_view(kr[:, t * RD:(t + 1) * RD], 1), head_view(lat[:, t, QL + KVL:LATW], 1), t - 1, 1)
            dve.tensor_copy(kr[:, 0:RD], lat[:, 0, QL + KVL:LATW]).then_inc(kr_done, 1)

            steps = [0]

            def conv(j, a, b):
                for k in range(a, b):
                    src, dst = zb[:, j + 1, k:k + CW], zb[:, j, 0:CW]
                    wk = cwt[:, CK * j + k:CK * j + k + 1]
                    if k == 0:
                        dve.wait_ge(z_done, j + 1)
                        if steps[0]:
                            dve.wait_ge(conv_step, steps[0])
                        ins = dve.tensor_scalar(dst, src, wk, vt[:, V_CB + j:V_CB + j + 1], ALU.mult, ALU.add)
                    else:
                        dve.wait_ge(conv_step, steps[0])
                        ins = dve.scalar_tensor_tensor(out=dst, in0=src, scalar=wk, in1=dst, op0=ALU.mult, op1=ALU.add)
                    ins.then_inc(conv_step, 1)
                    steps[0] += 1

            todo = [(j, k) for j in range(KD) for k in range(CK)]
            ready = [0]

            def conv_some(n):
                for _ in range(n):
                    if todo and todo[0][0] < ready[0]:
                        j, k = todo.pop(0)
                        conv(j, k, k + 1)

            dve.wait_ge(zpad_done, 1)
            for j in range(KD):
                split(item_no[("conv", j)] + 2)
                g = ("ca", j)
                p = got(dve, g)
                dve.wait_ge(sgc_done, j + 1)
                for a, b, o in ((0, TC, PAD), (TC, T, 2 * PAD + TC)):
                    ins = dve.tensor_tensor(zb[:, j + 1, o:o + b - a], p[:, a:b], sgc[:, j % 2, a:b], ALU.mult)
                ins.then_inc(z_done, 1)
                ready[0] = j + 1
                if j == 1:
                    for k in range(3):
                        p = got(dve, ("qnT", k))
                        dve.wait_ge(flo_done, KD + k - 1)
                        dve.tensor_scalar(ftmp[:, k % 2, :], p[:, 0:T], vt[:, V_QG + k:V_QG + k + 1], None,
                                          ALU.mult).then_inc(f_done, 1)
                        dve.wait_ge(fhi_done, KD + k + 1)
                        dve.tensor_tensor(qnl[:, k, :], ftmp[:, k % 2, :], qnh[:, k, :].bitcast(F32),
                                          ALU.subtract).then_inc(flo_done, 1)
                    for k in range(2):
                        p = got(dve, ("ckT", k))
                        dve.wait_ge(fhi_done, KD + 3 + k + 1)
                        dve.tensor_tensor(ckl[:, k, :], p[:, :], ckh[:, k, :].bitcast(F32),
                                          ALU.subtract).then_inc(flo_done, 1)
                conv_some(8)
            for j in range(8):
                split(item_no[("gate", j)] + 2)
                conv_some(11)
            def rotate_queries(h0, h1):
                for t in (1, 2):
                    v = qtok[:, t, :].rearrange("p (h e) -> p h e", h=H)[:, h0:h1, ND:HD]
                    v = v.rearrange("p h (a b f) -> p h a b f", a=2, b=2)
                    rope(v, v, t - 1, h1 - h0)

            for b in range(3):
                split(item_no[("uq", b)] + 2)
                if b < 2:
                    conv_some(6)
            early = 1024 // HD
            dve.wait_ge(qtok_done, 6)
            rotate_queries(0, early)
            dve.wait_ge(qtok_done, 9)
            rotate_queries(early, H)
            dve.tensor_copy(stat[:, 52:53], stat[:, 12:13]).then_inc(qrope_done, 1)
            split(item_no[("uk",)] + 2)
            conv_some(3)
            for h in range(1, H, 2):
                p = got(dve, ("qT", h))
                dve.tensor_copy(qT[:, h, :], p[0:HD, 0:T]).then_inc(qT_dve, 1)
            split(item_no[("uv",)] + 2)
            conv_some(10)
            for h in range(H + 1):
                if h < H:
                    for t in range(NT):
                        w = P if t == 0 else 384
                        g = ("s", h, t)
                        b, n = use[g]
                        dve.wait_ge(filled[b], n + 1)
                        if t == 0 and h >= 2:
                            dve.wait_ge(prn_done, h - 1)
                        link(dve, "v", dve.tensor_reduce(mx[:, h % 2, 8 + t:9 + t], psum[b][:, 0:w], AX, ALU.max))
                        dve.tensor_scalar(mx[:, h % 2, t:t + 1], mx[:, h % 2, 8 + t:9 + t], -SCALE, None,
                                          ALU.mult).then_inc(nmax_done, 1)
                if h >= 1:
                    hh = h - 1
                    dve.wait_ge(exp_done, NT * hh + NT)
                    link(dve, "v", dve.reciprocal(mx[:, hh % 2, 12:15], mx[:, hh % 2, 4:7]))
                    for t in range(NT):
                        a, w = (0, P) if t == 0 else (P + 384 * (t - 1), 384)
                        ins = dve.tensor_scalar(pr[:, hh % 3, a:a + w], pr[:, hh % 3, a:a + w],
                                                mx[:, hh % 2, 12 + t:13 + t], None, ALU.mult)
                    ins.then_inc(prn_done, 1)
                    split(item_no[("mod", 4 + hh // 2, hh % 2)] + 2)
                conv_some(5)
            while todo:
                conv_some(1)
            for k in range(KD):
                dve.wait_ge(ahi_done, k + 1)
                dve.tensor_tensor(aTl[:, k, :], aT[:, k, :], aTh[:, k, :].bitcast(F32), ALU.subtract).then_inc(alo_done, 1)

            def gated(k):
                p = got(dve, ("wo", k))
                dve.tensor_tensor(m[:, k, :], p[:, 0:T], siga[:, k, :], ALU.mult).then_inc(m_done, 1)

            p = got(dve, ("mean",))
            dve.wait_ge(conv_step, steps[0])
            for k in range(KD):
                dve.scalar_tensor_tensor(out=zb[:, k, 0:CW], in0=p[:, 0:CW], scalar=-1.0 / D, in1=zb[:, k, 0:CW],
                                         op0=ALU.mult, op1=ALU.add).then_inc(cen_done, 1)
            split(item_no[("wo", 0)] + 2)
            dve.wait_ge(alo_done, KD)
            dve.wait_ge(siga_in, 16)
            gated(0)
            gated(1)
            split(item_no[("wo", 1)] + 2)
            p = got(dve, ("var",))
            dve.tensor_scalar(sq[:, 0, :], p[:, 0:CW], 1.0 / D, EPS, ALU.mult, ALU.add).then_inc(lnv_done, 1)
            dve.wait_ge(lns_done, 1)
            link(dve, "v", dve.reciprocal(lnr[:, :], sq[:, 1, :]))
            for k in range(KD):
                dve.tensor_tensor(zb[:, k, 0:CW], zb[:, k, 0:CW], lnr[:, :], ALU.mult).then_inc(zn_done, 1)
                if k:
                    dve.wait_ge(znh_done, k)
                    dve.tensor_tensor(znl[:, k - 1, :], zf[:, (k - 1) % 2, :], znh[:, k - 1, :].bitcast(F32),
                                      ALU.subtract).then_inc(znl_done, 1)
            dve.wait_ge(znh_done, KD)
            dve.tensor_tensor(znl[:, KD - 1, :], zf[:, (KD - 1) % 2, :], znh[:, KD - 1, :].bitcast(F32),
                              ALU.subtract).then_inc(znl_done, 1)
            gated(2)
            gated(3)
            for j in (2, 3):
                split(item_no[("wo", j)] + 2)
                gated(2 * j)
                gated(2 * j + 1)
            dve.wait_ge(sigc_in, 16)
            for j in range(4):
                split(item_no[("pw2", j)] + 2)
                for k in (2 * j, 2 * j + 1):
                    p = got(dve, ("pw2", k))
                    link(dve, "v", dve.tensor_tensor(mt[:, k % 2, :], p[:, 0:T], sigc[:, k, :], ALU.mult))
                    dve.tensor_tensor(m[:, k, :], m[:, k, :], mt[:, k % 2, :], ALU.add).then_inc(m_done, 1)
                    dve.wait_ge(mh_done, k + 1)
                    dve.tensor_tensor(ml[:, k, :], m[:, k, :], mh[:, k, :].bitcast(F32), ALU.subtract).then_inc(ml_done, 1)
            dve.wait_ge(g2row_in, 16)
            for cc in range(2):
                for b in range(2):
                    g = ("bc", 4, cc, b)
                    p = got(dve, g)
                    dve.scalar_tensor_tensor(out=a2[:, cc, 512 * b:512 * b + 512], in0=p[:, :], scalar=1.0,
                                             in1=g2row[:, 512 * b:512 * b + 512], op0=ALU.add,
                                             op1=ALU.mult).then_inc(bc_v, 1)
            def normed2(t):
                dve.wait_ge(ssq2_done, t + 1)
                dve.tensor_scalar(stat[:, 44 + t:45 + t], stat[:, 40 + t:41 + t], 1.0 / D, EPS, ALU.mult, ALU.add).then_inc(r2v, 1)
                dve.wait_ge(r2a, t + 1)
                link(dve, "v", dve.reciprocal(stat[:, 48 + t:49 + t], stat[:, 48 + t:49 + t]))
                v = h2p[:, t, :].rearrange("t (c p) -> t p c", c=KD)
                cc = cond_of(t)
                link(dve, "v", dve.scalar_tensor_tensor(out=v, in0=x1[:, t, :].rearrange("t (p c) -> t p c", c=KD),
                                                        scalar=stat[:, 48 + t:49 + t],
                                                        in1=a2[:, cc, :].rearrange("t (p c) -> t p c", c=KD),
                                                        op0=ALU.mult, op1=ALU.mult))
                dve.tensor_tensor(v, v, b2[:, cc, :].rearrange("t (p c) -> t p c", c=KD), ALU.add).then_inc(h2_done, 1)

            dve.wait_ge(xr_in, 32)
            dve.wait_ge(bc_a, 8)
            for b in range(2):
                split(item_no[("wout", b, 0)] + 2)
                split(item_no[("wout", b, 1)] + 2)
                for t in range(NT):
                    p = got(dve, ("wout", b, t))
                    cols = slice(512 * b, 512 * b + 512)
                    if NT * b + t >= 2:
                        dve.wait_ge(x1_done, NT * b + t - 1)
                    u = (NT * b + t) % 2
                    link(dve, "v", dve.tensor_tensor(xt[:, u, :], p[:, :], g1[:, cond_of(t), cols], ALU.mult))
                    dve.tensor_tensor(x1[:, t, cols], x1[:, t, cols], xt[:, u, :], ALU.add).then_inc(x1_done, 1)
                    if b and t:
                        normed2(t - 1)
            normed2(NT - 1)
            for k in range(KD):
                p = got(dve, ("h2T", k))
                dve.wait_ge(h2h_done, k + 1)
                dve.tensor_tensor(h2l[:, k, :], p[:, 0:T], h2h[:, k, :].bitcast(F32), ALU.subtract).then_inc(h2l_done, 1)
            split(item_no[("router",)] + 2)
            split(item_no[("shgu", 0)] + 2)
            dve.wait_ge(rsc_done, NT)
            link(dve, "v", dve.tensor_tensor(rsel[:, :, :], rsc[:, :, :],
                                             rbias[:, :].unsqueeze(1).to_broadcast([P, NT, NE]), ALU.add))
            link(dve, "v", dve.memset(rgs[:, :, :], -2e38))
            for t in range(NT):
                for g in range(NG):
                    ins = dve.max(rg8[:, t, g, :], rsel[:, t, 8 * g:8 * g + 8])
            link(dve, "v", ins)
            link(dve, "v", dve.tensor_tensor(rgs[:, :, 0:NG], rg8[:, :, :, 0], rg8[:, :, :, 1], ALU.add))
            for t in range(NT):
                ins = dve.max(rt8[:, t, :], rgs[:, t, :])
            link(dve, "v", ins)
            link(dve, "v", dve.memset(rt8[:, :, 4:8], -2e38))
            for t in range(NT):
                ins = dve.match_replace(rgr[:, t, :], rt8[:, t, :], rgs[:, t, :], -3e38)
            link(dve, "v", ins)
            link(dve, "v", dve.tensor_tensor(rgm[:, :, :], rgr[:, :, 0:NG], rgs[:, :, 0:NG], ALU.is_equal))
            link(dve, "v", dve.tensor_scalar(rgm[:, :, :], rgm[:, :, :], -1e30, None, ALU.mult))
            selv = rsel[:, :, :].rearrange("p t (g e) -> p (t g) e", e=8)
            link(dve, "v", dve.tensor_tensor(selv, selv,
                                             rgm[:, :, :].rearrange("p t g -> p (t g)").unsqueeze(2)
                                             .to_broadcast([P, NT * NG, 8]), ALU.add))
            for t in range(NT):
                ins = dve.max(rk8[:, t, :], rsel[:, t, :])
            link(dve, "v", ins)
            for t in range(NT):
                ins = dve.match_replace(rtmp[:, t, :], rk8[:, t, :], rsel[:, t, :], -3e38)
            link(dve, "v", ins)
            dve.tensor_tensor(rmsk[:, :, :], rtmp[:, :, :], rsel[:, :, :], ALU.not_equal).then_inc(mask_done, 1)
            dve.wait_ge(mask_done, 1)
            for t in range(NT):
                link(dve, "v", dve.tensor_tensor(rsc[:, t, :], rsc[:, t, :], rmsk[:, t, :], ALU.mult))
                link(dve, "v", dve.tensor_reduce(rsum[:, t:t + 1], rsc[:, t, :], AX, ALU.add))
            link(dve, "v", dve.reciprocal(rsum[:, :], rsum[:, :]))
            for t in range(NT):
                ins = dve.tensor_tensor_scan(rrk[:, t, :], ones[:, 0:NE], rmsk[:, t, :], 0.0, ALU.mult, ALU.add)
            link(dve, "v", ins)
            link(dve, "v", dve.tensor_tensor(rrk[:, :, :], rrk[:, :, :], rmsk[:, :, :], ALU.subtract))
            for t in range(NT):
                link(dve, "v", dve.tensor_scalar(rgs[:, t, 0:1], token[:, t:t + 1], float(TOPK), -BIG, ALU.mult, ALU.add))
                link(dve, "v", dve.tensor_scalar(rgs[:, t, 1:2], token[:, t:t + 1], -BIG, None, ALU.add))
                for r in range(ROUNDS):
                    v = vals[:, t, NE * r:NE * r + NE, :]
                    dve.tensor_scalar(v[:, :, 0], rmsk[:, t, :], 0.0, rgs[:, t, 1:2], ALU.mult, ALU.add)
                    dve.tensor_scalar(v[:, :, 1], rrk[:, t, :], rgs[:, t, 0:1], None, ALU.add)
                    link(dve, "v", dve.tensor_scalar(v[:, :, 2], rsc[:, t, :], rsum[:, t:t + 1], 2.5, ALU.mult, ALU.mult))
            for t in range(NT):
                g = ("shgu", t)
                p = got(dve, g)
                dve.wait_ge(shs_done, t + 1)
                dve.tensor_tensor(shh[:, t, :], p[:, FF:2 * FF], shs[:, t, :], ALU.mult).then_inc(shh_done, 1)
            for t in range(NT):
                p = got(dve, ("pos", t))
                link(dve, "v", dve.tensor_scalar(rtmp[:, t, :], rmsk[:, t, :], -1000.0, 1000.0, ALU.mult, ALU.add))
                for r in range(ROUNDS):
                    dve.scalar_tensor_tensor(out=pos3[:, t, NE * r:NE * r + NE], in0=p[:, 0:NE], scalar=float(-P * r),
                                             in1=rtmp[:, t, :], op0=ALU.add, op1=ALU.add).then_inc(pos_done, 1)
            p = got(dve, ("cnt",))
            link(dve, "v", dve.tensor_reduce(rounds_f[:, 0:1], p[:, 0:NE], AX, ALU.max))
            link(dve, "v", dve.tensor_scalar(rounds_f[:, 1:2], rounds_f[:, 0:1], float(P), 1.0, ALU.is_gt, ALU.add))
            link(dve, "v", dve.tensor_scalar(rounds_f[:, 2:3], rounds_f[:, 0:1], float(2 * P), None, ALU.is_gt))
            link(dve, "v", dve.tensor_tensor(rounds_f[:, 3:4], rounds_f[:, 1:2], rounds_f[:, 2:3], ALU.add))
            dve.tensor_scalar(rounds_i[:, :], rounds_f[:, 3:4], float(NE // 4), -2.0, ALU.mult, ALU.add).then_inc(rtab_done, 1)
            def xsplit(i, k, q):
                j, s = i * 4 + k, 3 * (k % 2) + q
                dve.wait_ge(xhi_done, 3 * j + (q + 1))
                if q < 2:
                    src = raw[s][:, :].rearrange("p (w k n) -> p k w n", w=2, k=4)
                    h, l = (v[s][:, :].rearrange("p (k w n) -> p k w n", w=2, k=4) for v in (hi, lo))
                else:
                    src, h, l = raw[s][:, :], hi[s][:, :], lo[s][:, :]
                dve.tensor_tensor(l, src, h.bitcast(F32), ALU.subtract).then_inc(xlo_done, 1)

            for t in range(NT):
                g = ("shT", t)
                p = got(dve, g)
                dve.wait_ge(shTh_done, t + 1)
                dve.tensor_tensor(shTl[:, t, :], p[:, 0:FF], shTh[:, t, :].bitcast(F32),
                                  ALU.subtract).then_inc(shTl_done, 1)
                if t < 2:
                    xsplit(0, 0, t)
            for t in range(NT):
                for b in range(2):
                    n, cols = 2 * t + b, slice(512 * b, 512 * b + 512)
                    p = got(dve, ("shd", t, b))
                    if n >= 2:
                        dve.wait_ge(shared_added, n - 1)
                    link(dve, "v", dve.tensor_tensor(shg[:, n % 2, :], p[:, :], g2[:, cond_of(t), cols], ALU.mult))
                    dve.tensor_tensor(x1[:, t, cols], x1[:, t, cols], shg[:, n % 2, :], ALU.add).then_inc(shared_added, 1)

            dve.wait_ge(rtab_done, 1)
            last = dve.value_load(rounds_i[0:1, 0:1], min_val=NE // 4 - 2, max_val=ROUNDS * NE // 4 - 2) + 1

            def turn_lo(i, k):
                j = i * 4 + k
                for b in range(2):
                    dve.wait_ge(xgh_done, 2 * j + (b + 1))
                    dve.tensor_tensor(xgl[k % 2][:, 4 * b:4 * b + 4, :],
                                      psum[2 + b][:, :].rearrange("p (k n) -> p k n", k=4),
                                      xgh[k % 2][:, 4 * b:4 * b + 4, :].bitcast(F32), ALU.subtract).then_inc(xgl_done, 1)

            def list_of(i, k):
                j = i * 4 + k
                dve.wait_ge(list_filled, j + 1)
                if not isinstance(j, int) or j >= 4:
                    dve.wait_ge(ixs_done, j - 3)
                dve.tensor_scalar(ixt[k % 4][:, :], psum[5][:, 0:2], BIG, None, ALU.add)
                dve.tensor_copy(gsl[k % 4][:, :], psum[5][:, 2:3]).then_inc(list_done, 1)

            def rows_out(i, k):
                j = i * 4 + k
                dve.wait_ge(dn_filled, j + 1)
                if not isinstance(j, int) or j >= 2:
                    dve.wait_ge(scattered[k % 2], uses(i, k - 2) * 16)
                dve.tensor_copy(ys[k % 2][:, 512:D], psum[7][:, :]).then_inc(yv_done, 1)

            def step(i, k, left=9):
                j = i * 4 + k
                early = isinstance(j, int) and j < 1
                if left > 2:
                    list_of(i, k + 2)
                if left > 1:
                    turn_lo(i, k + 1)
                    xsplit(i, k + 1, 0)
                    xsplit(i, k + 1, 1)
                dve.wait_ge(sg_done, j + 1)
                if not early:
                    dve.wait_ge(ht_filled, j)
                dve.scalar_tensor_tensor(out=hd[:, :], in0=psum[k % 2][:, FF:2 * FF], scalar=gsl[k % 4][:, :],
                                         in1=sg[:, :], op0=ALU.mult, op1=ALU.mult).then_inc(hd_done, 1)
                if left > 1:
                    xsplit(i, k + 1, 2)
                if not early:
                    rows_out(i, k - 1)
                dve.wait_ge(hdh_done, j + 1)
                dve.tensor_tensor(hdl[k % 2][:, :], psum[4][:, 0:FF], hdh[k % 2][:, :].bitcast(F32),
                                  ALU.subtract).then_inc(hdl_done, 1)

            list_of(0, 0)
            list_of(0, 1)
            xsplit(0, 0, 2)
            turn_lo(0, 0)
            for k in range(4):
                step(0, k)
            with dve.Fori(1, last) as i:
                for k in range(4):
                    step(i, k)
            for k in range(4):
                step(last, k, left=4 - k)
            rows_out(last, 3)

            def summed(n):
                t, b = n // 2, n % 2
                cols, cc, sl = slice(512 * b, 512 * b + 512), cond_of(t), slots[n % 4]
                ts = tsum[t % 2][:, cols]
                dve.wait_ge(slots_in[n % 4], 16 * (n // 4 + 1))
                if n >= 4:
                    dve.wait_ge(tss_done, n - 3)
                    dve.wait_ge(y_done, t - 1)
                for w in (4, 2):
                    link(dve, "v", dve.tensor_tensor(sl[:, 0:w, :], sl[:, 0:w, :], sl[:, w:2 * w, :], ALU.add))
                dve.tensor_tensor(ts, sl[:, 0, :], sl[:, 1, :], ALU.add).then_inc(tsum_done, 1)
                dve.wait_ge(tsum_done, n + 1)
                dve.wait_ge(tail_in, 32)
                link(dve, "v", dve.tensor_tensor(ts, ts, tg[:, cc, cols], ALU.mult))
                dve.wait_ge(tx_in[t % 2], 16 * (t // 2 + 1))
                dve.tensor_tensor(ts, ts, tx[t % 2][:, cols], ALU.add).then_inc(t2_done, 1)

            def normed(t):
                dve.wait_ge(tss_done, 2 * t + 2)
                link(dve, "v", dve.tensor_tensor(stat[:, 54 + t:55 + t], stat[:, 16 + 2 * t:17 + 2 * t],
                                                 stat[:, 17 + 2 * t:18 + 2 * t], ALU.add))
                dve.tensor_scalar(stat[:, 57 + t:58 + t], stat[:, 54 + t:55 + t], 1.0 / D, EPS, ALU.mult, ALU.add).then_inc(trv, 1)
                dve.wait_ge(tra, t + 1)
                link(dve, "v", dve.reciprocal(stat[:, 60 + t:61 + t], stat[:, 60 + t:61 + t]))
                if t >= 2:
                    dve.wait_ge(y_out[t % 2], 16 * (t // 2))
                dve.scalar_tensor_tensor(out=tout[t % 2][:, :], in0=tsum[t % 2][:, :], scalar=stat[:, 60 + t:61 + t],
                                         in1=fgr[:, :], op0=ALU.mult, op1=ALU.mult).then_inc(y_done, 1)

            for n in range(2 * NT):
                summed(n)
                if n >= 2 and n % 2 == 0:
                    normed(n // 2 - 1)
            normed(NT - 1)

        @block.tensor
        def _(pe):
            order = iter(groups)

            def begin(g):
                assert next(order) == g, g
                b, n = use[g]
                if n:
                    pe.wait_ge(*read_by(groups[8 * (n - 1) + b]))
                return psum[b]

            def end(g, ins):
                ins.then_inc(filled[use[g][0]], 1)

            def mm3(out, ah, al, bh, bl, first, last):
                pe.matmul(out, ah, bh, start=first, stop=False)
                pe.matmul(out, ah, bl, start=False, stop=False)
                return pe.matmul(out, al, bh, start=False, stop=last)

            def item(n):
                pe.wait_ge(lo_done, item_no[n] + 1)
                return hl(n)

            def turn(out, src):
                n = src.shape[0]
                return pe.transpose(out, src, ident[0:n, 0:n])

            def mod_half(p, b, h):
                wh, wl = item(("mod", b, h))
                for k in range(4):
                    c4 = cst[:, 4 * (4 * h + k):4 * (4 * h + k) + 4]
                    pe.matmul(p[0:4, :], c4, wh[:, k, :], start=(h == 0 and k == 0), stop=False)
                    ins = pe.matmul(p[0:4, :], c4, wl[:, k, :], start=False, stop=(h == 1 and k == 3))
                if h == 0:
                    ins.then_inc(half_used, 1)
                else:
                    end(("mod", b), ins)

            pe.wait_ge(rows_in, 16 * 9)
            p = begin(("vt",))
            end(("vt",), turn(p[:, 0:51], vrow[0:51, :]))
            p = begin(("cw",))
            for k in range(KD):
                ins = turn(p[:, CK * k:CK * k + CK], cwrow[:, P * k:P * k + P])
            end(("cw",), ins)
            pe.wait_ge(cst_done, 4)
            for b in range(4):
                p = begin(("mod", b))
                for h in range(2):
                    mod_half(p, b, h)
            pe.wait_ge(mod_done, 4)
            pe.wait_ge(biasrow1_in, 16)
            p = begin(("modc",))
            for v in range(2):
                for k in range(KD):
                    ins = pe.matmul(p[:, 2 * (KD * v + k):2 * (KD * v + k) + 2],
                                    modr1[0:5, D * v + P * k:D * v + P * k + P], cst_of("pick", 5),
                                    start=True, stop=True)
            end(("modc",), ins)
            pe.wait_ge(xn_done, NT)
            for k in range(KD):
                p = begin(("hT", k))
                for t in range(NT):
                    ins = turn(p[:, P * t:P * t + P], xn[:, t, P * k:P * k + P])
                end(("hT", k), ins)
            for b in range(2):
                ps = [begin(("lat", b, t)) for t in range(NT)]
                for h in range(2):
                    wh, wl = item(("lat", b, h))
                    for t in range(NT):
                        for k in range(4):
                            kk = 4 * h + k
                            if b == 0 and t == 0:
                                pe.wait_ge(flo_done, kk + 1)
                            ins = mm3(ps[t][:, 0:336], hTh[:, kk, P * t:P * t + P], hTl[:, kk, P * t:P * t + P],
                                      wh[:, k, :], wl[:, k, :], kk == 0, kk == 7)
                        if h:
                            end(("lat", b, t), ins)
                    if not h:
                        ins.then_inc(half_used, 1)

            def by_channel(g, wh, wl, col, ah, al):
                p = begin(g)
                for k in range(KD):
                    ins = mm3(p[:, 0:T], wh[:, k, col:col + P], wl[:, k, col:col + P], ah[:, k, :], al[:, k, :],
                              k == 0, k == KD - 1)
                end(g, ins)

            for j in range(KD):
                wh, wl = item(("conv", j))
                by_channel(("ca", j), wh, wl, 0, hTh, hTl)
                by_channel(("cg", j), wh, wl, P, hTh, hTl)
                if j == 1:
                    pe.wait_ge(latn_done, 2 * NT)
                    for k in range(3):
                        p = begin(("qnT", k))
                        for t in range(NT):
                            ins = turn(p[:, P * t:P * t + P], lat[:, t, P * k:P * k + P])
                        end(("qnT", k), ins)
                    pe.wait_ge(small_in, 64)
                    for k in range(2):
                        p = begin(("ckT", k))
                        for t in range(4):
                            ins = turn(p[:, P * t:P * t + P], lat[:, t, QL + P * k:QL + P * k + P])
                        end(("ckT", k), ins)
            for j in range(KD):
                wh, wl = item(("gate", j))
                for b in range(2):
                    by_channel(("gl", 2 * j + b), wh, wl, P * b, hTh, hTl)
            pe.wait_ge(flo_done, KD + 5)
            for b in range(3):
                wh, wl = item(("uq", b))
                for t in range(NT):
                    p = begin(("uq", b, t))
                    for k in range(3):
                        ins = mm3(p[:, :], qnh[:, k, P * t:P * t + P], qnl[:, k, P * t:P * t + P],
                                  wh[:, k, :], wl[:, k, :], k == 0, k == 2)
                    end(("uq", b, t), ins)
            pe.wait_ge(kr_done, 1)
            p = begin(("krT",))
            for t in range(4):
                ins = turn(p[0:RD, P * t:P * t + P], kr[:, RD * t:RD * t + RD])
            end(("krT",), ins)
            wh, wl = item(("uk",))
            for i in range(8):
                p = begin(("uk", i))
                for k in range(2):
                    ins = mm3(p[:, :], wh[:, k, P * i:P * i + P], wl[:, k, P * i:P * i + P],
                              ckh[:, k, :], ckl[:, k, :], k == 0, k == 1)
                end(("uk", i), ins)
            pe.wait_ge(qtok_done, 9)
            pe.wait_ge(qrope_done, 1)
            for h in range(H):
                p = begin(("qT", h))
                for t in range(NT):
                    ins = turn(p[0:HD, P * t:P * t + P], qtok[:, t, HD * h:HD * h + HD])
                end(("qT", h), ins)
            wh, wl = item(("uv",))
            for kt in range(4):
                for b in range(2):
                    p = begin(("uv", kt, b))
                    for k in range(2):
                        ins = mm3(p[:, :], ckh[:, k, P * kt:P * kt + P], ckl[:, k, P * kt:P * kt + P],
                                  wh[:, k, 512 * b:512 * b + 512], wl[:, k, 512 * b:512 * b + 512], k == 0, k == 1)
                    end(("uv", kt, b), ins)

            pe.wait_ge(kT_done, H)
            pe.wait_ge(krep_done, 1)
            pe.wait_ge(qT_act, H // 2)
            pe.wait_ge(qT_dve, H // 2)
            for h in range(H + 3):
                if h < H:
                    for t in range(NT):
                        keys = slice(0, P) if t == 0 else slice(P, 4 * P)
                        g = ("s", h, t)
                        p = begin(g)
                        end(g, pe.matmul(p[:, 0:keys.stop - keys.start], qT[:, h, P * t:P * t + P], kT[:, h, keys],
                                         start=True, stop=True))
                if h >= 3:
                    hh = h - 3
                    if hh % 2 == 0:
                        pv = begin(("pv", hh // 2))
                    if hh == 0:
                        pe.wait_ge(v_done, 8)
                    pe.wait_ge(pTa_done, hh + 1)
                    pe.wait_ge(pTv_done, hh + 1)
                    r = slice(VD * (hh % 2), VD * (hh % 2) + VD)
                    for kt in (1, 2, 3):
                        pe.matmul(pv[r, P:T], V[:, kt, VD * hh:VD * hh + VD], pT[:, 256 * (kt - 1):256 * kt],
                                  start=(kt == 1), stop=(kt == 3))
                    ins = pe.matmul(pv[r, 0:P], V[:, 0, VD * hh:VD * hh + VD], pT[:, 768:896], start=True, stop=True)
                    if hh % 2:
                        end(("pv", hh // 2), ins)
                    else:
                        ins.then_inc(pv_half, 1)
                if h < H:
                    if h % 2 == 0:
                        pmod = begin(("mod", 4 + h // 2))
                    mod_half(pmod, 4 + h // 2, h % 2)
                if 2 <= h < H + 2:
                    hh = h - 2
                    pe.wait_ge(prn_done, hh + 1)
                    pA = begin(("pT", hh, 0))
                    for kt in (1, 2):
                        for t in (1, 2):
                            a = P + 384 * (t - 1) + P * (kt - 1)
                            o = 256 * (kt - 1) + P * (t - 1)
                            ins = turn(pA[:, o:o + P], pr[:, hh % 3, a:a + P])
                    end(("pT", hh, 0), ins)
                    pB = begin(("pT", hh, 1))
                    for t in (1, 2):
                        a = P + 384 * (t - 1) + 256
                        turn(pB[:, P * (t - 1):P * t], pr[:, hh % 3, a:a + P])
                    end(("pT", hh, 1), turn(pB[:, 256:384], pr[:, hh % 3, 0:P]))

            pe.wait_ge(conv_step, KD * CK)
            p = begin(("mean",))
            for k in range(KD):
                ins = pe.matmul(p[:, 0:CW], ones, zb[:, k, 0:CW], start=(k == 0), stop=(k == KD - 1))
            end(("mean",), ins)
            pe.wait_ge(alo_done, KD)
            for j in range(4):
                wh, wl = item(("wo", j))
                for b in range(2):
                    by_channel(("wo", 2 * j + b), wh, wl, P * b, aTh, aTl)
                if j == 0:
                    p = begin(("var",))
                    for k in range(KD):
                        pe.wait_ge(sq_done, k + 1)
                        ins = pe.matmul(p[:, 0:CW], ones, sq[:, k % 2, :], start=(k == 0), stop=(k == KD - 1))
                        if k < KD - 1:
                            ins.then_inc(var_step, 1)
                    end(("var",), ins)
            pe.wait_ge(znl_done, KD)
            for j in range(4):
                wh, wl = item(("pw2", j))
                for b in range(2):
                    by_channel(("pw2", 2 * j + b), wh, wl, P * b, znh, znl)
            pe.wait_ge(mod_done, 12)
            pe.wait_ge(biasrow2_in, 16)
            a, _ = at["pick_rows"]

            def rows_of(v):
                for cc in range(2):
                    for b in range(2):
                        g = ("bc", v, cc, b)
                        p = begin(g)
                        o = D * (v - 2) + 512 * b
                        end(g, pe.matmul(p[:, :], con[0:5, a + P * cc:a + P * cc + P], modr2[0:5, o:o + 512],
                                         start=True, stop=True))

            rows_of(2)
            rows_of(4)
            rows_of(3)
            pe.wait_ge(ml_done, KD)
            for b in range(2):
                ps = [begin(("wout", b, t)) for t in range(NT)]
                for h in range(2):
                    wh, wl = item(("wout", b, h))
                    for t in range(NT):
                        for k in range(4):
                            kk = 4 * h + k
                            ins = mm3(ps[t][:, :], mh[:, kk, P * t:P * t + P], ml[:, kk, P * t:P * t + P],
                                      wh[:, k, :], wl[:, k, :], kk == 0, kk == 7)
                        if h:
                            end(("wout", b, t), ins)
                    if not h:
                        ins.then_inc(half_used, 1)
            rows_of(5)
            pe.wait_ge(h2_done, NT)
            for k in range(KD):
                p = begin(("h2T", k))
                for t in range(NT):
                    ins = turn(p[:, P * t:P * t + P], h2p[:, t, P * k:P * k + P])
                end(("h2T", k), ins)
            pe.wait_ge(h2l_done, KD)
            wh, wl = item(("router",))
            for t in range(NT):
                p = begin(("rt", t))
                for k in range(KD):
                    ins = mm3(p[:, 0:NE], h2h[:, k, P * t:P * t + P], h2l[:, k, P * t:P * t + P],
                              wh[:, k, :], wl[:, k, :], k == 0, k == KD - 1)
                end(("rt", t), ins)
            ps = [begin(("shgu", t)) for t in range(NT)]
            for h in range(2):
                wh, wl = item(("shgu", h))
                for t in range(NT):
                    for k in range(4):
                        kk = 4 * h + k
                        ins = mm3(ps[t][:, :], h2h[:, kk, P * t:P * t + P], h2l[:, kk, P * t:P * t + P],
                                  wh[:, k, :], wl[:, k, :], kk == 0, kk == 7)
                    if h:
                        end(("shgu", t), ins)
                if not h:
                    ins.then_inc(half_used, 1)
            pe.wait_ge(mask_done, 1)
            for t in range(NT):
                p = begin(("pos", t))
                for s in range(t):
                    pe.matmul(p[:, 0:NE], ones, rmsk[:, s, :], start=(s == 0), stop=False)
                end(("pos", t), pe.matmul(p[:, 0:NE], before, rmsk[:, t, :], start=(t == 0), stop=True))
            p = begin(("cnt",))
            for t in range(NT):
                ins = pe.matmul(p[:, 0:NE], ones, rmsk[:, t, :], start=(t == 0), stop=(t == NT - 1))
            end(("cnt",), ins)
            for t in range(NT):
                pe.wait_ge(shh_done, t + 1)
                p = begin(("shT", t))
                v = shh[:, t, :].rearrange("t (p c) -> t c p", c=2)
                for k in range(2):
                    ins = turn(p[:, P * k:P * k + P], v[:, k, :])
                end(("shT", t), ins)
            for t in range(NT):
                wh, wl = item(("shd",))
                pe.wait_ge(shTl_done, t + 1)
                for b in range(2):
                    p = begin(("shd", t, b))
                    for k in range(2):
                        ins = mm3(p[:, :], shTh[:, t, P * k:P * k + P], shTl[:, t, P * k:P * k + P],
                                  wh[:, k, 512 * b:512 * b + 512], wl[:, k, 512 * b:512 * b + 512], k == 0, k == 1)
                    end(("shd", t, b), ins)

            for g in groups[-8:]:
                pe.wait_ge(*read_by(g))
            pe.wait_ge(rtab_done, 1)
            last = pe.value_load(rounds_i[0:1, 0:1], min_val=NE // 4 - 2, max_val=ROUNDS * NE // 4 - 2) + 1

            def token_list(i, k):
                j = i * 4 + k
                pe.wait_ge(oh_done, j + 1)
                if not isinstance(j, int) or j >= 1:
                    pe.wait_ge(list_done, j)
                for t in range(NT):
                    rhs = vals[:, t, j, :] if isinstance(j, int) else vals[:, t, bass.ds(j, 1), :].rearrange("p a n -> p (a n)")
                    ins = pe.matmul(psum[5][:, 0:3], oh[k % 2][:, t, :], rhs, start=(t == 0), stop=(t == NT - 1))
                ins.then_inc(list_filled, 1)

            def turn_tokens(i, k):
                j = i * 4 + k
                pe.wait_ge(gathered[k % 2], uses(i, k) * 16)
                if not isinstance(j, int) or j >= 1:
                    pe.wait_ge(xgl_done, 2 * j)
                for q in range(KD):
                    ins = turn(psum[2 + q // 4][:, P * (q % 4):P * (q % 4) + P], xg[k % 2][:, P * q:P * q + P])
                ins.then_inc(xt_filled, 1)

            def gate_up(i, k):
                j = i * 4 + k
                pe.wait_ge(xgl_done, 2 * j + 2)
                if not isinstance(j, int) or j >= 2:
                    pe.wait_ge(hd_done, j - 1)
                for q in range(2):
                    s = 3 * (k % 2) + q
                    pe.wait_ge(xlo_done, 3 * j + (q + 1))
                    wh, wl = (v[s][:, :].rearrange("p (k n) -> p k n", k=4) for v in (hi, lo))
                    for c4 in range(4):
                        kk = 4 * q + c4
                        ins = mm3(psum[k % 2][:, :], xgh[k % 2][:, kk, :], xgl[k % 2][:, kk, :],
                                  wh[:, c4, :], wl[:, c4, :], kk == 0, kk == 7)
                ins.then_inc(gu_filled, 1)

            def down(i, k):
                j, s = i * 4 + k, 3 * (k % 2) + 2
                pe.wait_ge(hdl_done, j + 1)
                pe.wait_ge(xlo_done, 3 * j + 3)
                if not isinstance(j, int) or j >= 1:
                    pe.wait_ge(ya_done, j)
                    pe.wait_ge(yv_done, j)
                wh, wl = (v[s][:, :].rearrange("p (k n) -> p k n", k=2) for v in (hi, lo))
                for b in range(2):
                    for c2 in range(2):
                        ins = mm3(psum[6 + b][:, :], hdh[k % 2][:, P * c2:P * c2 + P], hdl[k % 2][:, P * c2:P * c2 + P],
                                  wh[:, c2, 512 * b:512 * b + 512], wl[:, c2, 512 * b:512 * b + 512], c2 == 0, c2 == 1)
                ins.then_inc(dn_filled, 1)

            def turn_hidden(i, k):
                j = i * 4 + k
                pe.wait_ge(hd_done, j + 1)
                if not isinstance(j, int) or j >= 1:
                    pe.wait_ge(hdl_done, j)
                v = hd[:, :].rearrange("t (p c) -> t c p", c=2)
                for c2 in range(2):
                    ins = turn(psum[4][:, P * c2:P * c2 + P], v[:, c2, :])
                ins.then_inc(ht_filled, 1)

            def step(i, k, left=9):
                if left > 2:
                    token_list(i, k + 2)
                if left > 1:
                    turn_tokens(i, k + 1)
                gate_up(i, k)
                if not isinstance(i, int) or 4 * i + k > 0:
                    down(i, k - 1)
                turn_hidden(i, k)

            token_list(0, 0)
            token_list(0, 1)
            turn_tokens(0, 0)
            for k in range(4):
                step(0, k)
            with pe.Fori(1, last) as i:
                for k in range(4):
                    step(i, k)
            for k in range(4):
                step(last, k, left=4 - k)
            down(last, 3)


_INS = ["x_prompt", "x_sample", "cache_ckv", "cache_krope", "c", "c_ctx", "mod_w", "mod_b", "norm1_g", "w_in",
        "q_norm_g", "w_uq", "kv_norm_g", "w_ukv", "w_o_attn", "conv_w", "conv_b", "conv_ln_g", "conv_ln_b", "w_pw2",
        "w_out", "norm2_g", "router_w", "router_bias", "exp_w_gate", "exp_w_up", "exp_w_down",
        "sh_w_gate", "sh_w_up", "sh_w_down", "final_g"]
_OUTS = [(1, TC, D), (1, T - TC, D), (1, 1, TC, KVL), (1, 1, TC, RD)]


def kernel(**inputs):
    import numpy as _np
    import concourse.bacc as _bacc
    from concourse.bass_utils import run_bass_kernel_spmd as _run

    nc = _bacc.Bacc("TRN2", target_bir_lowering=False, num_devices=1)
    table, at = constants()
    arrays, args = {}, []
    for name in _INS:
        a = _np.ascontiguousarray(inputs[name])
        arrays[f"in_{name}_dram"] = a
        args.append(nc.dram_tensor(f"in_{name}_dram", a.shape, mybir.dt.from_np(a.dtype), kind="ExternalInput").ap())
    arrays["in_constants_dram"] = _np.ascontiguousarray(table)
    consts = nc.dram_tensor("in_constants_dram", table.shape, F32, kind="ExternalInput").ap()
    outs = [nc.dram_tensor(f"out_{i}_dram", shape, F32, kind="ExternalOutput").ap() for i, shape in enumerate(_OUTS)]
    hybrid_step(nc, *args, consts, at, *outs)
    r = _run(nc, [arrays], core_ids=[0])
    return tuple(r.results[0][f"out_{i}_dram"] for i in range(len(_OUTS)))
```
